# Optimizing a Trainium2 kernel written in Bass

```python
import jax, jax.numpy as jnp
from jax import lax
import numpy as np

D_MODEL = 2048
BATCH = 1
SEQ = 256
DEPTH = 1
DEC_BATCH = 1
DEC_SEQ = 256
PAST_LEN = 128

HEAD_DIM = 128
EPS = 1e-6
QBLOCK = 128
GRID_W = 64
A_GROUPS = ((128, 1), (512, 4), (2048, 16))
A_HEADS_PER_GROUP = 4
A_HEADS = A_HEADS_PER_GROUP * len(A_GROUPS)
A_WIDTH = A_HEADS * HEAD_DIM
A_OUT = A_HEADS_PER_GROUP * HEAD_DIM
ROPE_THETA_A = 500000.0
ROT_A = HEAD_DIM // 4
B_Q_HEADS = 8
B_KV_HEADS = 2
B_Q_WIDTH = B_Q_HEADS * HEAD_DIM
B_KV_WIDTH = B_KV_HEADS * HEAD_DIM
ROPE_THETA_B = 10000.0
AXIAL_HALF = HEAD_DIM // 2
IN_SPLITS = (A_WIDTH, A_WIDTH, A_WIDTH, B_Q_WIDTH, B_KV_WIDTH, B_KV_WIDTH, D_MODEL, D_MODEL)
IN_WIDTH = sum(IN_SPLITS)
PEER_HEADS = 8
PEER_NKEYS = 128
PEER_EXPERTS = PEER_NKEYS * PEER_NKEYS
PEER_QDIM = 256
PEER_TOPK = 16
PEER_CHUNK = 128

kernel_name = "hybrid_dilated_axial_peer_encoder"

def rms_norm(x, g):
    xf = x.astype(jnp.float32)
    y = xf * lax.rsqrt(jnp.mean(xf * xf, axis=-1, keepdims=True) + EPS)
    return (y * g.astype(jnp.float32)).astype(x.dtype)

def rope_cos_sin(pos, dim, theta):
    inv = theta ** (-(jnp.arange(0, dim, 2, dtype=jnp.float32) / dim))
    ang = pos.astype(jnp.float32)[:, None] * inv[None, :]
    return jnp.cos(ang), jnp.sin(ang)

def apply_rope(x, cos, sin):
    xf = x.astype(jnp.float32)
    x1, x2 = jnp.split(xf, 2, axis=-1)
    c = cos[None, :, None, :]
    s = sin[None, :, None, :]
    return jnp.concatenate([x1 * c - x2 * s, x2 * c + x1 * s], axis=-1).astype(x.dtype)

def banded_attention(q, k, v, half):
    n, length, nh, dh = q.shape
    nb = -(-length // QBLOCK)
    lp = nb * QBLOCK
    kw = QBLOCK + 2 * half
    qp = jnp.pad(q, ((0, 0), (0, lp - length), (0, 0), (0, 0)))
    kp = jnp.pad(k, ((0, 0), (half, lp - length + half), (0, 0), (0, 0)))
    vp = jnp.pad(v, ((0, 0), (half, lp - length + half), (0, 0), (0, 0)))
    kidx = jnp.arange(nb)[:, None] * QBLOCK + jnp.arange(kw)[None, :]
    kb = kp[:, kidx]
    vb = vp[:, kidx]
    qb = qp.reshape(n, nb, QBLOCK, nh, dh)
    s = jnp.einsum('nbqhd,nbkhd->nbhqk', qb, kb).astype(jnp.float32) * (dh ** -0.5)
    key_pos = kidx - half
    q_pos = jnp.arange(nb)[:, None] * QBLOCK + jnp.arange(QBLOCK)[None, :]
    rel = key_pos[:, None, :] - q_pos[:, :, None]
    key_ok = (key_pos[:, None, :] >= 0) & (key_pos[:, None, :] < length)
    mask = (jnp.abs(rel) <= half) & (key_ok | (q_pos[:, :, None] >= length))
    s = jnp.where(mask[None, :, None], s, -jnp.inf)
    lse = jax.nn.logsumexp(s, axis=-1)
    p = jnp.exp(s - lse[..., None]).astype(v.dtype)
    o = jnp.einsum('nbhqk,nbkhd->nbqhd', p, vb).reshape(n, lp, nh, dh)[:, :length]
    lse = lse.transpose(0, 1, 3, 2).reshape(n, lp, nh)[:, :length]
    return o, lse

def dilated_group(q, k, v, window, dilation):
    bn, length, nh, dh = q.shape
    ls = length // dilation
    half = (window // 2) // dilation

    def to_res(t):
        return t.reshape(bn, ls, dilation, nh, dh).transpose(0, 2, 1, 3, 4).reshape(bn * dilation, ls, nh, dh)

    o, lse = banded_attention(to_res(q), to_res(k), to_res(v), half)
    o = o.reshape(bn, dilation, ls, nh, dh).transpose(0, 2, 1, 3, 4).reshape(bn, length, nh, dh)
    lse = lse.reshape(bn, dilation, ls, nh).transpose(0, 2, 1, 3).reshape(bn, length, nh)
    return o, lse

def gqa_dense_blocked(q, k, v):
    bn, length, hq, dh = q.shape
    hkv = k.shape[2]
    grp = hq // hkv
    nb = length // QBLOCK
    qb = q.reshape(bn, nb, QBLOCK, hkv, grp, dh).transpose(1, 0, 2, 3, 4, 5)
    scale = dh ** -0.5

    def one_block(qblk):
        s = jnp.einsum('bqkgd,bskd->bkgqs', qblk, k).astype(jnp.float32) * scale
        p = jax.nn.softmax(s, axis=-1).astype(v.dtype)
        return jnp.einsum('bkgqs,bskd->bqkgd', p, v)

    o = lax.map(one_block, qb)
    return o.transpose(1, 0, 2, 3, 4, 5).reshape(bn, length, hq * dh)

def peer(h, w_pq, sub_keys, u_emb, v_emb):
    bn, length, d = h.shape
    t = bn * length
    ht = h.reshape(t, d)
    q = (ht @ w_pq).reshape(t, PEER_HEADS, 2, PEER_QDIM // 2)
    s = jnp.einsum('thcd,hcnd->thcn', q, sub_keys).astype(jnp.float32)
    v1, i1 = lax.top_k(s[:, :, 0], PEER_TOPK)
    v2, i2 = lax.top_k(s[:, :, 1], PEER_TOPK)
    cand = (v1[..., :, None] + v2[..., None, :]).reshape(t, PEER_HEADS, PEER_TOPK * PEER_TOPK)
    cv, ci = lax.top_k(cand, PEER_TOPK)
    e = (jnp.take_along_axis(i1, ci // PEER_TOPK, axis=-1) * PEER_NKEYS
         + jnp.take_along_axis(i2, ci % PEER_TOPK, axis=-1))
    g = jax.nn.softmax(cv, axis=-1)
    nc = t // PEER_CHUNK
    sel = PEER_HEADS * PEER_TOPK

    def chunk(args):
        hc, ec, gc = args
        a = jnp.einsum('ckd,cd->ck', u_emb[ec], hc)
        coef = (jax.nn.gelu(a.astype(jnp.float32), approximate=False) * gc).astype(v_emb.dtype)
        return jnp.einsum('ck,ckd->cd', coef, v_emb[ec])

    out = lax.map(chunk, (ht.reshape(nc, PEER_CHUNK, d), e.reshape(nc, PEER_CHUNK, sel),
                          g.reshape(nc, PEER_CHUNK, sel)))
    return out.reshape(bn, length, d).astype(h.dtype)

def encoder_layer(x, g_mix, w_in, qn_a, kn_a, qn_b, kn_b, w_br_a, w_br_b, w_out,
                  g_ffn, w_pq, sub_keys, u_emb, v_emb):
    bn, length, _ = x.shape
    h = rms_norm(x, g_mix)
    proj = h @ w_in
    cuts = [int(c) for c in np.cumsum(IN_SPLITS)[:-1]]
    qa, ka, va, qb, kb, vb, ga, gb = jnp.split(proj, cuts, axis=-1)

    qa = rms_norm(qa.reshape(bn, length, A_HEADS, HEAD_DIM), qn_a)
    ka = rms_norm(ka.reshape(bn, length, A_HEADS, HEAD_DIM), kn_a)
    va = va.reshape(bn, length, A_HEADS, HEAD_DIM)
    cos_a, sin_a = rope_cos_sin(jnp.arange(length), ROT_A, ROPE_THETA_A)
    qa = jnp.concatenate([apply_rope(qa[..., :ROT_A], cos_a, sin_a), qa[..., ROT_A:]], axis=-1)
    ka = jnp.concatenate([apply_rope(ka[..., :ROT_A], cos_a, sin_a), ka[..., ROT_A:]], axis=-1)
    outs, lses = [], []
    for gi, (window, dilation) in enumerate(A_GROUPS):
        hs = slice(gi * A_HEADS_PER_GROUP, (gi + 1) * A_HEADS_PER_GROUP)
        o_g, l_g = dilated_group(qa[:, :, hs], ka[:, :, hs], va[:, :, hs], window, dilation)
        outs.append(o_g)
        lses.append(l_g)
    wts = jax.nn.softmax(jnp.stack(lses, axis=0), axis=0)
    oa = jnp.sum(wts[..., None].astype(va.dtype) * jnp.stack(outs, axis=0), axis=0)
    oa = oa.reshape(bn, length, A_OUT)

    rows = length // GRID_W
    row_ids = jnp.repeat(jnp.arange(rows), GRID_W)
    col_ids = jnp.tile(jnp.arange(GRID_W), rows)
    cos_r, sin_r = rope_cos_sin(row_ids, AXIAL_HALF, ROPE_THETA_B)
    cos_c, sin_c = rope_cos_sin(col_ids, AXIAL_HALF, ROPE_THETA_B)

    def axial(t):
        return jnp.concatenate([apply_rope(t[..., :AXIAL_HALF], cos_r, sin_r),
                                apply_rope(t[..., AXIAL_HALF:], cos_c, sin_c)], axis=-1)

    qb = axial(rms_norm(qb.reshape(bn, length, B_Q_HEADS, HEAD_DIM), qn_b))
    kb = axial(rms_norm(kb.reshape(bn, length, B_KV_HEADS, HEAD_DIM), kn_b))
    vb = vb.reshape(bn, length, B_KV_HEADS, HEAD_DIM)
    ob = gqa_dense_blocked(qb, kb, vb)

    merged = jax.nn.sigmoid(ga) * (oa @ w_br_a) + jax.nn.sigmoid(gb) * (ob @ w_br_b)
    x = x + merged @ w_out

    x = x + peer(rms_norm(x, g_ffn), w_pq, sub_keys, u_emb, v_emb)
    return x

def setup_inputs(seed: int = 0) -> dict:
    key = jax.random.key(seed)
    ks = jax.random.split(key, 16)
    f32 = jnp.float32

    def nrm(k, shape, scale):
        return jax.random.normal(k, shape, f32) * scale

    def gain(k, shape):
        return 1.0 + 0.02 * jax.random.normal(k, shape, f32)

    return {
        "x_prompt": jax.random.normal(ks[0], (BATCH, SEQ, D_MODEL), f32),
        "x_sample": jax.random.normal(ks[1], (DEC_BATCH, DEC_SEQ, D_MODEL), f32),
        "g_mix": gain(ks[2], (DEPTH, D_MODEL)),
        "w_in": nrm(ks[3], (DEPTH, D_MODEL, IN_WIDTH), D_MODEL ** -0.5),
        "qn_a": gain(ks[4], (DEPTH, HEAD_DIM)),
        "kn_a": gain(ks[5], (DEPTH, HEAD_DIM)),
        "qn_b": gain(ks[6], (DEPTH, HEAD_DIM)),
        "kn_b": gain(ks[7], (DEPTH, HEAD_DIM)),
        "w_br_a": nrm(ks[8], (DEPTH, A_OUT, D_MODEL), A_OUT ** -0.5),
        "w_br_b": nrm(ks[9], (DEPTH, B_Q_WIDTH, D_MODEL), B_Q_WIDTH ** -0.5),
        "w_out": nrm(ks[10], (DEPTH, D_MODEL, D_MODEL), D_MODEL ** -0.5),
        "g_ffn": gain(ks[11], (DEPTH, D_MODEL)),
        "w_pq": nrm(ks[12], (DEPTH, D_MODEL, PEER_HEADS * PEER_QDIM), D_MODEL ** -0.5),
        "sub_keys": nrm(ks[13], (DEPTH, PEER_HEADS, 2, PEER_NKEYS, PEER_QDIM // 2), (PEER_QDIM // 2) ** -0.5),
        "u_emb": nrm(ks[14], (DEPTH, PEER_EXPERTS, D_MODEL), D_MODEL ** -0.5),
        "v_emb": nrm(ks[15], (DEPTH, PEER_EXPERTS, D_MODEL), PEER_HEADS ** -0.5),
    }

def reference(x_prompt, x_sample, g_mix, w_in, qn_a, kn_a, qn_b, kn_b, w_br_a, w_br_b, w_out,
              g_ffn, w_pq, sub_keys, u_emb, v_emb):
    y_prompt = x_prompt
    y_sample = x_sample
    for l in range(DEPTH):
        y_prompt = encoder_layer(y_prompt, g_mix[l], w_in[l], qn_a[l], kn_a[l], qn_b[l], kn_b[l],
                                 w_br_a[l], w_br_b[l], w_out[l], g_ffn[l], w_pq[l], sub_keys[l],
                                 u_emb[l], v_emb[l])
        y_sample = encoder_layer(y_sample, g_mix[l], w_in[l], qn_a[l], kn_a[l], qn_b[l], kn_b[l],
                                 w_br_a[l], w_br_b[l], w_out[l], g_ffn[l], w_pq[l], sub_keys[l],
                                 u_emb[l], v_emb[l])
    return (y_prompt, y_sample)


_drawn_inputs = setup_inputs


def setup_inputs(seed=0):
    import zlib

    import numpy as np

    out = dict(_drawn_inputs(seed))
    spreads = {}
    factors = {'g_mix': 5.079, 'qn_a': 7.549, 'kn_a': 6.558, 'qn_b': 8.0, 'kn_b': 8.0, 'g_ffn': 8.0}
    for name, (base, spread) in spreads.items():
        noise = np.random.default_rng([zlib.crc32(name.encode()), seed]).standard_normal(out[name].shape)
        drawn = base * np.exp(spread * noise) if base else spread * noise
        out[name] = __import__('jax').numpy.asarray(drawn.astype(out[name].dtype))
    for name, factor in factors.items():
        out[name] = (out[name] * factor).astype(out[name].dtype)
    return out
```

```python
import numpy as np
import concourse.bass as bass
from concourse import mybir

F32 = mybir.dt.float32
F32R = mybir.dt.float32r
U32 = mybir.dt.uint32
ALU = mybir.AluOpType
ACT = mybir.ActivationFunctionType
AX = mybir.AxisListType

P = 128
D = 2048
KC = D // P
TOK = 256
NT = TOK // P
REQ = 2
DH = 128
SCALE = DH ** -0.5
EPS = 1e-6
CT = 512
SK = 4
SPC = KC // SK
RING = 4
A_HEADS, A_MERGED, A_GROUPS = 12, 4, 3
B_HEADS, B_KV = 8, 2
QKV_CT = 12
GATE_CT = 8
ROT = 16
PH, NKEYS, TOPK = 8, 128, 16
SEL = PH * TOPK
NEG = -1.0e30
LOWEST = -3.0e38


QK_TILES = (0, 1, 2, 3, 4, 5, 9, 10, 11)
N_UNITS = 16
N_OUT = 12


def out_of(u):
    return u // 2 if u < 8 else u - 4


class Counter:

    def __init__(self, sem):
        self.sem, self.n = sem, 0

    def after(self, eng, ins):
        self.n += 1
        ins.then_inc(self.sem, 1)
        eng.wait_ge(self.sem, self.n)


def encoder(nc, x, g_mix_b, g_ffn_b, w_in, gains, w_br_a, w_br_b, w_out, w_pq, sub_keys, u_emb, v_emb,
            ident_c, mask_c, rope_a_c, rope_b_c, iota_c, y):
    base = 16512
    place = {}

    def at(name, offset, shape, dtype):
        place[name] = nc.alloc_sbuf_tensor_at(name, [P] + shape, dtype, offset=offset)
        return place[name]

    o = base
    ident = at("ident", o, [P], F32); o += 512
    rope_a = at("rope_a", o, [2, NT, ROT], F32); o += 256
    rope_b = at("rope_b", o, [2, NT, 2, 32], F32); o += 1024
    gain = at("gain", o, [4, DH], F32); o += 2048
    mask = at("mask", o, [NT, A_GROUPS * TOK], F32); o += 6144
    iota = at("iota", o, [TOPK], F32); o += 64
    tick = at("tick", o, [2], F32); o += 32
    stat = at("stat", o, [64], F32); o += 256
    R_HT = o; o += 32768
    R_RAW = o; o += 49152
    R_QKT = o; o += 34816
    R_W = o; o += 32768
    R_SPLIT = o; o += 32768
    R_H2 = o; o += 16384

    ht_hi = at("ht_hi", R_HT, [KC, TOK], F32R)
    ht_lo = at("ht_lo", R_HT + 16384, [KC, TOK], F32R)
    raw = at("raw", R_RAW, [QKV_CT, NT, CT], F32)
    ot_hi = at("ot_hi", R_RAW, [12, TOK], F32R)
    ot_lo = at("ot_lo", R_RAW + 12288, [12, TOK], F32R)
    xin = at("xin", R_RAW, [NT, D], F32)
    x1 = at("x1", R_RAW + 16384, [NT, D], F32)
    gvec = at("gvec", R_RAW + 32768, [D], F32)
    junk = at("junk", R_RAW + 40960, [D], F32)
    qkt = at("qkt", R_QKT, [34, TOK], F32)
    sg = at("sg", R_QKT, [2 * KC, TOK], F32)
    skn = at("skn", R_QKT, [2 * PH, P], F32)
    skt = at("skt", R_QKT + 8192, [2 * PH, P], F32)
    qt = at("qt", R_QKT + 16384, [2 * PH, TOK], F32)
    w = at("w", R_W, [RING, SK, CT], F32)
    w_hi = at("w_hi", R_SPLIT, [2, SK, CT], F32R)
    w_lo = at("w_lo", R_SPLIT + 16384, [2, SK, CT], F32R)
    h2 = at("h2", R_H2, [NT, D], F32)
    prob = at("prob", R_SPLIT, [2, A_GROUPS * TOK], F32)
    pt = at("pt", R_SPLIT + 6144, [2, 6, TOK], F32)
    sq = at("sq", R_SPLIT + 18432, [2 * CT], F32)
    rt = at("rt", R_SPLIT + 22528, [4, 384], F32)
    ss = at("ss", R_SPLIT + 28672, [72], F32)
    rs = at("rs", R_SPLIT + 28960, [72], F32)
    rtmp = at("rtmp", R_SPLIT + 29248, [72], F32)
    ust = at("ust", R_SPLIT + 29536, [N_UNITS, 8], F32)
    m1 = at("m1", R_RAW + 24576, [4, TOK], F32)
    m2 = at("m2", R_RAW + 28672, [4, TOK], F32)
    s = at("s", R_RAW, [NT, 2 * PH, NKEYS], F32)
    cand = at("cand", R_RAW + 16384, [PH, TOPK * TOPK], F32)
    eq = at("eq", R_RAW + 24576, [PH * TOPK, TOPK], F32)
    topv = at("topv", R_RAW + 32768, [2 * PH, TOPK], F32)
    topi = at("topi", R_RAW + 33792, [2 * PH, TOPK], U32)
    topf = at("topf", R_RAW + 34816, [2 * PH, TOPK], F32)
    cv = at("cv", R_RAW + 35840, [PH, TOPK], F32)
    ci = at("ci", R_RAW + 36352, [PH, TOPK], U32)
    cpart = at("cpart", R_RAW + 36864, [SEL], U32)
    cpf = at("cpf", R_RAW + 37376, [SEL], F32)
    e1 = at("e1", R_RAW + 37888, [SEL], F32)
    e2 = at("e2", R_RAW + 38400, [SEL], F32)
    gsum = at("gsum", R_RAW + 38912, [PH], F32)
    eidx = at("eidx", R_SPLIT, [NT * SEL + 8], U32)
    gsel = at("gsel", R_SPLIT + 1088, [NT, SEL], F32)
    dots = at("dots", R_SPLIT + 2112, [NT, SEL], F32)
    coef = at("coef", R_SPLIT + 3136, [NT, SEL], F32)
    stage_i = at("stage_i", R_SPLIT + 4160, [8], U32)
    stage_d = at("stage_d", R_SPLIT + 4192, [8], F32)
    dump = at("dump", R_SPLIT + 4224, [2, D], F32)
    rows = at("rows", R_RAW, [8, D], F32)
    acc = at("acc", R_HT, [NT, D], F32)

    ps = nc.alloc_psum_tensor("ps", [P, 8, 512], F32)
    S = nc.alloc_semaphore
    consts_in = S("consts_in")
    x_in, g_in, xres_in, g2_in, sk_in, y_out, x1_back = (S(n) for n in ("x_in", "g_in", "xres_in", "g2_in", "sk_in", "y_out", "x1_back"))
    w_loaded = [S(f"w_loaded{j}") for j in range(RING)]
    hi_ready, lo_ready, slab_done = S("hi_ready"), S("lo_ready"), S("slab_done")
    acc_free = S("acc_free")
    done = {n: S(f"done_{n}") for n in ("pe", "act", "dve", "pool")}
    act_own, dve_own = S("act_own"), S("dve_own")
    dotted, summed, ticked = S("dotted"), S("summed"), S("ticked")
    sum_ready, mean_ready, root_ready = S("sum_ready"), S("mean_ready"), S("root_ready")
    normed, turned, turn_hi, turn_lo = S("normed"), S("turned"), S("turn_hi"), S("turn_lo")
    squared, sq_free, roped, qk_turned, qk_out = S("squared"), S("sq_free"), S("roped"), S("qk_turned"), S("qk_out")
    sc_ready, sc_max, exp_done, p_ready, p_turned, pt_ready, pv_ready, o_hi, o_lo = (
        S(n) for n in ("sc_ready", "sc_max", "exp_done", "p_ready", "p_turned", "pt_ready", "pv_ready", "o_hi", "o_lo"))
    merged, merged_hi = S("merged"), S("merged_hi")
    sk_turned, sk_out, s_ready, s_out, shifted, exped = (S(n) for n in ("sk_turned", "sk_out", "s_ready", "s_out", "shifted", "exped"))
    row_in = [S(f"row_in{j}") for j in range(8)]
    row_used, idx_ready, dots_done, gelu_done = S("row_used"), S("idx_ready"), S("dots_done"), S("gelu_done")

    def slabs(columns, slab_base, acc_base):
        return dict(pairs=columns // 2, g0=slab_base, a0=acc_base)

    phases, g, a = [], 0, 0
    for r in range(REQ):
        ph = {}
        for name, n in (("qkv", QKV_CT), ("gate", GATE_CT)):
            ph[name] = slabs(n, g, a); g += SPC * n; a += n
        ph["branch"] = dict(g0=g, a0=a); g += 12; a += 8
        for name, n in (("out", 4), ("pq", 4)):
            ph[name] = slabs(n, g, a); g += SPC * n; a += n
        phases.append(ph)

    w_view = {
        "qkv": (w_in.rearrange("(s k p) n -> s p k n", k=SK, p=P), 0),
        "gate": (w_in.rearrange("(s k p) n -> s p k n", k=SK, p=P), QKV_CT * CT),
        "out": (w_out.rearrange("(s k p) n -> s p k n", k=SK, p=P), 0),
        "pq": (w_pq.rearrange("(s k p) n -> s p k n", k=SK, p=P), 0),
    }
    bra = w_br_a.rearrange("(s k p) n -> s p k n", k=SK, p=P)
    brb = w_br_b.rearrange("(s k p) n -> s p k n", k=SK, p=P)

    def enter(eng, me, n):
        for other in done:
            if other != me and n:
                eng.wait_ge(done[other], n)

    def leave(eng, me):
        eng.drain().then_inc(done[me], 1)

    block_cm = nc.Block()
    with block_cm as block:

        @block.sync
        def _(sp):
            def load(src, slot, g_):
                if not isinstance(g_, int) or g_ >= RING:
                    sp.wait_ge(lo_ready, g_ - RING + 1)
                sp.dma_start(w[:, slot, :, :], src).then_inc(w_loaded[slot], 16)

            def stream(name, ph):
                view, col0 = w_view[name]

                def pair(i):
                    for c in range(2):
                        for j in range(SPC):
                            g_ = i * (2 * SPC) + (ph["g0"] + SPC * c + j)
                            n0 = i * (2 * CT) + (col0 + c * CT)
                            load(view[j, :, :, bass.ds(n0, CT)], j, g_)
                pair(0)
                with sp.Fori(1, ph["pairs"]) as i:
                    pair(i)

            for r in range(REQ):
                ph = phases[r]
                stream("qkv", ph["qkv"])
                stream("gate", ph["gate"])
                n = ph["branch"]["g0"]
                for ct in range(4):
                    for src in (bra[0], brb[0], brb[1]):
                        load(src[:, :, ct * CT:(ct + 1) * CT], n % RING, n)
                        n += 1
                stream("out", ph["out"])
                stream("pq", ph["pq"])

        @block.gpsimd
        def _(pool):
            for dst, src in ((ident[:, :], ident_c), (rope_a[:, :, :, :], rope_a_c), (rope_b[:, :, :, :, :], rope_b_c),
                             (gain[:, :, :], gains), (mask[:, :, :], mask_c), (iota[:, :], iota_c)):
                pool.dma_start(dst, src).then_inc(consts_in, 16)
            n = 0
            for r in range(REQ):
                xr = x[r].rearrange("(t p) d -> p t d", p=P)
                yr = y[r].rearrange("(t p) d -> p t d", p=P)
                enter(pool, "pool", n)
                pool.dma_start(xin[:, :, :], xr).then_inc(x_in, 16)
                pool.dma_start(gvec[:, :], g_mix_b).then_inc(g_in, 16)
                leave(pool, "pool"); n += 1
                for _ in range(4):
                    enter(pool, "pool", n); leave(pool, "pool"); n += 1
                enter(pool, "pool", n)
                pool.dma_start(xin[:, :, :], xr).then_inc(xres_in, 16)
                pool.dma_start(gvec[:, :], g_ffn_b).then_inc(g2_in, 16)
                leave(pool, "pool"); n += 1
                enter(pool, "pool", n)
                pool.dma_start(yr, x1[:, :, :]).then_inc(y_out, 16)
                pool.dma_start(skn[:, :, :], sub_keys.rearrange("c n d -> n c d")).then_inc(sk_in, 16)
                pool.wait_ge(y_out, 16 * (2 * r + 1))
                leave(pool, "pool"); n += 1
                enter(pool, "pool", n); leave(pool, "pool"); n += 1
                enter(pool, "pool", n)
                pool.dma_start(acc[:, :, :], yr).then_inc(x1_back, 16)
                for table in range(2):
                    emb = (u_emb, v_emb)[table]
                    first = 2 * r + table
                    with pool.Fori(0, NT * SEL // 8) as i:
                        for half in range(2):
                            pool.wait_ge(idx_ready, i * 2 + (first * NT * SEL // 4 + half + 1 + 2 * first))
                            pool.tensor_tensor(tick[:, half:half + 1], iota[:, 0:1], iota[:, 0:1], ALU.add).then_inc(ticked, 1)
                            for j in range(4 * half, 4 * half + 4):
                                pool.indirect_dma_start(rows[:, j, :], None, emb, bass.IndirectOffsetOnAxis(ap=stage_i[:, j:j + 1], axis=0)).then_inc(row_in[j], 16)
                pool.wait_ge(done["dve"], n + 1)
                pool.dma_start(yr, acc[:, :, :]).then_inc(y_out, 16)
                pool.wait_ge(y_out, 16 * (2 * r + 2))
                leave(pool, "pool"); n += 1

        @block.scalar
        def _(act):
            own = Counter(act_own)

            def split_hi(g_, j):
                act.wait_ge(w_loaded[j % RING], loads(g_, j))
                act.wait_ge(slab_done, g_ + 1)
                act.activation(w_hi[:, j % 2, :, :], w[:, j % RING, :, :], ACT.Copy).then_inc(hi_ready, 1)

            def loads(g_, j):
                return (g_ - (j % RING)) * (16 // RING) + 16

            def stream(ph, evacuate):
                def pair(i, first=False):
                    for c in range(2):
                        for j in range(SPC):
                            split_hi(i * (2 * SPC) + (ph["g0"] + SPC * c + j), j)
                            if j == 1 and not (first and c == 0):
                                out(i * 2 + (c - 1), 1 - c)

                def out(ct, side):
                    act.wait_ge(slab_done, ct * SPC + (ph["g0"] + SPC + 2))
                    evacuate(ct, side).then_inc(acc_free, 1)
                pair(0, True)
                with act.Fori(1, ph["pairs"]) as i:
                    pair(i)
                out(2 * ph["pairs"] - 1, 1)

            def normalise(k, m_):
                for t in range(NT):
                    if t:
                        act.wait_ge(sum_ready, NT * k + t)
                    act.activation(junk[:, :], (xin if k % 2 == 0 else x1)[:, t, :], ACT.Square,
                                   accum_out=stat[:, t:t + 1]).then_inc(sum_ready, 1)
                act.wait_ge(mean_ready, m_ + 1)
                act.activation(stat[:, 4:6], stat[:, 2:4], ACT.Sqrt).then_inc(root_ready, 1)
                for t in range(NT):
                    for q in range(4):
                        m = k * 8 + t * 4 + q
                        act.wait_ge(turned, m + 1)
                        act.activation(ht_hi[:, 4 * q:4 * q + 4, t * P:(t + 1) * P],
                                       ps[:, 4 + q, :].rearrange("p (k t) -> p k t", k=4), ACT.Copy).then_inc(turn_hi, 1)

            n = 0
            for r in range(REQ):
                ph = phases[r]
                enter(act, "act", n)
                act.wait_ge(x_in, 16 * (r + 1))
                normalise(2 * r, 3 * r)
                leave(act, "act"); n += 1

                enter(act, "act", n)
                stream(ph["qkv"], lambda ct, side: act.activation(
                    raw[:, bass.ds(ct, 1), :, :].rearrange("p a t c -> p (a t c)"),
                    ps[:, 2 * side:2 * side + 2, :].rearrange("p b c -> p (b c)"), ACT.Copy))
                leave(act, "act"); n += 1

                enter(act, "act", n)
                for u, c in enumerate(QK_TILES):
                    wid = CT if c < 11 else 256
                    if u:
                        act.wait_ge(sq_free, 9 * r + u)
                    act.activation(sq[:, 0:2 * wid].rearrange("p (t c) -> p t c", t=2), raw[:, c, :, 0:wid],
                                   ACT.Square).then_inc(squared, 1)
                act.wait_ge(mean_ready, 3 * r + 2)
                act.activation(rs[:, 0:68], ss[:, 0:68], ACT.Sqrt).then_inc(root_ready, 1)
                for u, c in enumerate(QK_TILES):
                    nh = 4 if c < 11 else 2
                    act.wait_ge(qk_turned, 9 * r + u + 1)
                    b0 = 4 * (u % 2)
                    act.activation(qkt[:, 4 * u:4 * u + nh, :],
                                   ps[:, b0:b0 + 2, :].rearrange("p b (h t) -> p (b h) t", h=2)[:, 0:nh, :],
                                   ACT.Copy).then_inc(qk_out, 1)
                for u in range(N_UNITS):
                    uu = N_UNITS * r + u
                    act.wait_ge(sc_max, uu + 1)
                    if u < 8:
                        act.activation(prob[:, u % 2, :], prob[:, u % 2, :], ACT.Exp, bias=ust[:, u, 2:3], scale=SCALE,
                                       accum_out=ust[:, u, 4:5]).then_inc(exp_done, 1)
                    else:
                        b0 = 2 * (u % 2)
                        for t in range(NT):
                            ins = act.activation(prob[:, u % 2, t * TOK:(t + 1) * TOK], ps[:, b0, t * TOK:(t + 1) * TOK],
                                                 ACT.Exp, bias=ust[:, u, 2 + t:3 + t], scale=SCALE,
                                                 accum_out=ust[:, u, 4 + t:5 + t])
                        ins.then_inc(exp_done, 1)
                    act.wait_ge(p_turned, uu + 1)
                    o_, oi = out_of(u), N_OUT * r + out_of(u)
                    t = u % 2
                    if o_ >= 2 and (u >= 8 or t == 0):
                        act.wait_ge(pv_ready, oi - 1)
                    if u < 8:
                        act.activation(pt[:, o_ % 2, :, t * P:(t + 1) * P],
                                       ps[:, 4:6, :].rearrange("p b c -> p (b c)")[:, 0:768].rearrange("p (k q) -> p k q", k=6),
                                       ACT.Copy).then_inc(pt_ready, 1)
                    else:
                        act.activation(pt[:, o_ % 2, 0:2, :], ps[:, 4, :].rearrange("p (k q) -> p k q", k=2),
                                       ACT.Copy).then_inc(pt_ready, 1)
                    if u >= 8 or t == 1:
                        act.wait_ge(pv_ready, oi + 1)
                        act.activation(ot_hi[:, o_, :], ps[:, 6 + o_ % 2, 0:TOK], ACT.Copy).then_inc(o_hi, 1)
                leave(act, "act"); n += 1

                enter(act, "act", n)
                stream(ph["gate"], lambda ct, side: act.activation(
                    sg[:, bass.ds(ct * 4, 4), :].rearrange("p a t -> p (a t)"),
                    ps[:, 2 * side:2 * side + 2, :].rearrange("p b c -> p (b c)"), ACT.Sigmoid))
                leave(act, "act"); n += 1

                enter(act, "act", n)
                for ct in range(4):
                    for k in range(3):
                        gg = ph["branch"]["g0"] + 3 * ct + k
                        split_hi(gg, gg % RING)
                    act.wait_ge(merged, 4 * r + ct + 1)
                    act.activation(ht_hi[:, 4 * ct:4 * ct + 4, :], m1[:, :, :], ACT.Copy).then_inc(merged_hi, 1)
                leave(act, "act"); n += 1

                enter(act, "act", n)
                for i in range(2 * ph["out"]["pairs"] * SPC):
                    split_hi(ph["out"]["g0"] + i, i % RING)
                act.wait_ge(acc_free, 2 + ph["out"]["a0"] + 4)
                normalise(2 * r + 1, 3 * r + 2)
                leave(act, "act"); n += 1

                enter(act, "act", n)
                for i in range(2 * ph["pq"]["pairs"] * SPC):
                    split_hi(ph["pq"]["g0"] + i, i % RING)
                    if i % SPC == 1 and i > SPC:
                        ct = i // SPC - 1
                        act.wait_ge(slab_done, ph["pq"]["g0"] + SPC * (ct + 1) + 2)
                        act.activation(qt[:, 4 * ct:4 * ct + 4, :].rearrange("p a t -> p (a t)"),
                                       ps[:, 2 * (ct % 2):2 * (ct % 2) + 2, :].rearrange("p b c -> p (b c)"),
                                       ACT.Copy).then_inc(acc_free, 1)
                act.wait_ge(slab_done, ph["pq"]["g0"] + SPC * 4 + 2)
                act.activation(qt[:, 12:16, :].rearrange("p a t -> p (a t)"),
                               ps[:, 2:4, :].rearrange("p b c -> p (b c)"), ACT.Copy).then_inc(acc_free, 1)
                for q in range(4):
                    act.wait_ge(sk_turned, 4 * r + q + 1)
                    act.activation(skt[:, 4 * q:4 * q + 4, :].rearrange("p a n -> p (a n)"), ps[:, 4 + q, :],
                                   ACT.Copy).then_inc(sk_out, 1)
                leave(act, "act"); n += 1

                enter(act, "act", n)
                for q in range(8):
                    act.wait_ge(s_ready, 8 * r + q + 1)
                    t, c = q // 4, q % 4
                    act.activation(s[:, t, 4 * c:4 * c + 4, :].rearrange("p a n -> p (a n)"), ps[:, q, :],
                                   ACT.Copy).then_inc(s_out, 1)
                for t in range(NT):
                    act.wait_ge(shifted, NT * r + t + 1)
                    act.activation(gsel[:, t, :], gsel[:, t, :], ACT.Exp).then_inc(exped, 1)
                leave(act, "act"); n += 1

                enter(act, "act", n)
                act.wait_ge(dots_done, r + 1)
                act.activation(coef[:, :, :], dots[:, :, :], ACT.Gelu).then_inc(gelu_done, 1)
                leave(act, "act"); n += 1

        @block.vector
        def _(dve):
            own = Counter(dve_own)

            def split_lo(g_, j):
                dve.wait_ge(hi_ready, g_ + 1)
                dve.tensor_tensor(w_lo[:, j % 2, :, :], w[:, j % RING, :, :], w_hi[:, j % 2, :, :].bitcast(F32),
                                  ALU.subtract).then_inc(lo_ready, 1)

            def stream(ph):
                with dve.Fori(0, ph["pairs"]) as i:
                    for j in range(2 * SPC):
                        split_lo(i * (2 * SPC) + (ph["g0"] + j), j)

            def inverse_root(mean, root, out, tmp):
                own.after(dve, dve.reciprocal(out, root))
                own.after(dve, dve.tensor_tensor(tmp, out, out, ALU.mult))
                own.after(dve, dve.tensor_tensor(tmp, tmp, mean, ALU.mult))
                own.after(dve, dve.tensor_scalar(tmp, tmp, -0.5, 1.5, ALU.mult, ALU.add))
                own.after(dve, dve.tensor_tensor(out, out, tmp, ALU.mult))

            def normalise(k, src, dst):
                dve.wait_ge(sum_ready, NT * (k + 1))
                dve.tensor_scalar(stat[:, 2:4], stat[:, 0:2], 1.0 / D, EPS, ALU.mult, ALU.add).then_inc(mean_ready, 1)
                dve.wait_ge(mean_ready, mean_count[0] + 1); mean_count[0] += 1
                dve.wait_ge(root_ready, root_count[0] + 1); root_count[0] += 1
                inverse_root(stat[:, 2:4], stat[:, 4:6], stat[:, 6:8], stat[:, 8:10])
                for t in range(NT):
                    dve.scalar_tensor_tensor(dst[:, t, :], src[:, t, :], stat[:, 6 + t:7 + t], gvec[:, :],
                                             ALU.mult, ALU.mult).then_inc(normed, 1)
                for t in range(NT):
                    for q in range(4):
                        dve.wait_ge(turn_hi, k * 8 + t * 4 + q + 1)
                        dve.tensor_tensor(ht_lo[:, 4 * q:4 * q + 4, t * P:(t + 1) * P],
                                          ps[:, 4 + q, :].rearrange("p (k t) -> p k t", k=4),
                                          ht_hi[:, 4 * q:4 * q + 4, t * P:(t + 1) * P].bitcast(F32),
                                          ALU.subtract).then_inc(turn_lo, 1)

            mean_count, root_count = [0], [0]
            n = 0
            dve.sem_inc(dotted, 2)
            dve.sem_inc(row_used, 1)
            dve.wait_ge(consts_in, 96)
            for r in range(REQ):
                ph = phases[r]
                enter(dve, "dve", n)
                dve.wait_ge(g_in, 16 * (r + 1))
                normalise(2 * r, xin, x1)
                leave(dve, "dve"); n += 1

                enter(dve, "dve", n)
                stream(ph["qkv"])
                leave(dve, "dve"); n += 1

                enter(dve, "dve", n)
                for u, c in enumerate(QK_TILES):
                    nh = 8 if c < 11 else 4
                    dve.wait_ge(squared, 9 * r + u + 1)
                    dve.tensor_reduce(ss[:, 8 * u:8 * u + nh], sq[:, 0:nh * DH].rearrange("p (h d) -> p h d", d=DH),
                                      AX.X, ALU.add).then_inc(sq_free, 1)
                dve.wait_ge(sq_free, 9 * (r + 1))
                dve.tensor_scalar(ss[:, 0:68], ss[:, 0:68], 1.0 / DH, EPS, ALU.mult, ALU.add).then_inc(mean_ready, 1)
                dve.wait_ge(mean_ready, mean_count[0] + 1); mean_count[0] += 1
                dve.wait_ge(root_ready, root_count[0] + 1); root_count[0] += 1
                own.after(dve, dve.tensor_copy(rtmp[:, 0:68], rs[:, 0:68]))
                own.after(dve, dve.reciprocal(rs[:, 0:68], rtmp[:, 0:68]))
                own.after(dve, dve.tensor_tensor(rtmp[:, 0:68], rs[:, 0:68], rs[:, 0:68], ALU.mult))
                own.after(dve, dve.tensor_tensor(rtmp[:, 0:68], rtmp[:, 0:68], ss[:, 0:68], ALU.mult))
                own.after(dve, dve.tensor_scalar(rtmp[:, 0:68], rtmp[:, 0:68], -0.5, 1.5, ALU.mult, ALU.add))
                own.after(dve, dve.tensor_tensor(rs[:, 0:68], rs[:, 0:68], rtmp[:, 0:68], ALU.mult))
                for u, c in enumerate(QK_TILES):
                    nh = 4 if c < 11 else 2
                    gi = 0 if c < 3 else 1 if c < 6 else 2 if c < 11 else 3
                    for t in range(NT):
                        for h in range(nh):
                            v = raw[:, c, t, h * DH:(h + 1) * DH]
                            i = 8 * u + nh * t + h
                            ins = dve.scalar_tensor_tensor(v, v, rs[:, i:i + 1], gain[:, gi, :], ALU.mult, ALU.mult)
                own.after(dve, ins)

                def rotate(first, second, cos, sin, tmp):
                    dve.tensor_tensor(tmp(0), first, cos, ALU.mult)
                    dve.tensor_tensor(tmp(1), second, sin, ALU.mult)
                    dve.tensor_tensor(tmp(2), second, cos, ALU.mult)
                    own.after(dve, dve.tensor_tensor(tmp(3), first, sin, ALU.mult))
                    dve.tensor_tensor(first, tmp(0), tmp(1), ALU.subtract)
                    ins = dve.tensor_tensor(second, tmp(2), tmp(3), ALU.add)
                    own.after(dve, ins)

                for c in range(6):
                    for t in range(NT):
                        v = raw[:, c, t, :].rearrange("p (h d) -> p h d", d=DH)
                        cs = [rope_a[:, k, t, :].unsqueeze(1).to_broadcast([P, 4, ROT]) for k in range(2)]
                        rotate(v[:, :, 0:ROT], v[:, :, ROT:2 * ROT], cs[0], cs[1],
                               lambda k: rt[:, k, 0:64].rearrange("p (h d) -> p h d", d=ROT))
                for c in (9, 10, 11):
                    nh = 4 if c < 11 else 2
                    for t in range(NT):
                        for half in range(2):
                            v = raw[:, c, t, 0:nh * DH].rearrange("p (h d) -> p h d", d=DH)[:, :, 64 * half:64 * half + 64]
                            cs = [rope_b[:, k, t, half, :].unsqueeze(1).to_broadcast([P, nh, 32]) for k in range(2)]
                            rotate(v[:, :, 0:32], v[:, :, 32:64], cs[0], cs[1],
                                   lambda k: rt[:, k, 0:nh * 32].rearrange("p (h d) -> p h d", d=32))
                dve.drain().then_inc(roped, 1)
                for u in range(N_UNITS):
                    uu = N_UNITS * r + u
                    dve.wait_ge(sc_ready, uu + 1)
                    b0 = 2 * (u % 2)
                    if uu >= 2:
                        dve.wait_ge(p_turned, uu - 1)
                    if u < 8:
                        t = u % 2
                        own.after(dve, dve.tensor_tensor_reduce(
                            out=prob[:, u % 2, :], in0=ps[:, b0:b0 + 2, :].rearrange("p b c -> p (b c)")[:, 0:768],
                            in1=mask[:, t, :], scale=1.0, scalar=LOWEST, op0=ALU.add, op1=ALU.max, accum_out=ust[:, u, 0:1]))
                        dve.tensor_scalar(ust[:, u, 2:3], ust[:, u, 0:1], -SCALE, None, ALU.mult).then_inc(sc_max, 1)
                        dve.wait_ge(exp_done, uu + 1)
                        own.after(dve, dve.reciprocal(ust[:, u, 6:7], ust[:, u, 4:5]))
                        dve.tensor_scalar(prob[:, u % 2, :], prob[:, u % 2, :], ust[:, u, 6:7], None, ALU.mult).then_inc(p_ready, 1)
                    else:
                        own.after(dve, dve.tensor_reduce(ust[:, u, 0:2], ps[:, b0, :].rearrange("p (t k) -> p t k", t=NT), AX.X, ALU.max))
                        dve.tensor_scalar(ust[:, u, 2:4], ust[:, u, 0:2], -SCALE, None, ALU.mult).then_inc(sc_max, 1)
                        dve.wait_ge(exp_done, uu + 1)
                        own.after(dve, dve.reciprocal(ust[:, u, 6:8], ust[:, u, 4:6]))
                        for t in range(NT):
                            ins = dve.tensor_scalar(prob[:, u % 2, t * TOK:(t + 1) * TOK], prob[:, u % 2, t * TOK:(t + 1) * TOK],
                                                    ust[:, u, 6 + t:7 + t], None, ALU.mult)
                        ins.then_inc(p_ready, 1)
                    if u >= 8 or u % 2 == 1:
                        o_ = out_of(u)
                        dve.wait_ge(o_hi, N_OUT * r + o_ + 1)
                        dve.tensor_tensor(ot_lo[:, o_, :], ps[:, 6 + o_ % 2, 0:TOK], ot_hi[:, o_, :].bitcast(F32),
                                          ALU.subtract).then_inc(o_lo, 1)
                leave(dve, "dve"); n += 1

                enter(dve, "dve", n)
                stream(ph["gate"])
                leave(dve, "dve"); n += 1

                enter(dve, "dve", n)
                for ct in range(4):
                    for k in range(3):
                        gg = ph["branch"]["g0"] + 3 * ct + k
                        split_lo(gg, gg % RING)
                    for side in range(2):
                        dve.wait_ge(slab_done, ph["branch"]["g0"] + 3 * ct + (1, 3)[side] + 2)
                        if ct and side == 0:
                            dve.wait_ge(merged_hi, 4 * r + ct)
                        dve.tensor_tensor((m1, m2)[side][:, :, :].rearrange("p a t -> p (a t)"),
                                          ps[:, 2 * side:2 * side + 2, :].rearrange("p b c -> p (b c)"),
                                          sg[:, KC * side + 4 * ct:KC * side + 4 * ct + 4, :].rearrange("p a t -> p (a t)"),
                                          ALU.mult).then_inc(acc_free, 1)
                    dve.wait_ge(acc_free, 2 + ph["branch"]["a0"] + 2 * ct + 2)
                    dve.tensor_tensor(m1[:, :, :], m1[:, :, :], m2[:, :, :], ALU.add).then_inc(merged, 1)
                    dve.wait_ge(merged_hi, 4 * r + ct + 1)
                    dve.tensor_tensor(ht_lo[:, 4 * ct:4 * ct + 4, :], m1[:, :, :], ht_hi[:, 4 * ct:4 * ct + 4, :].bitcast(F32), ALU.subtract)
                leave(dve, "dve"); n += 1

                enter(dve, "dve", n)
                dve.wait_ge(xres_in, 16 * (r + 1))
                dve.wait_ge(g2_in, 16 * (r + 1))

                def residual(ct):
                    dve.wait_ge(slab_done, ph["out"]["g0"] + SPC * (ct + 1) + 2)
                    dve.tensor_tensor(x1[:, :, ct * CT:(ct + 1) * CT], ps[:, 2 * (ct % 2):2 * (ct % 2) + 2, :],
                                      xin[:, :, ct * CT:(ct + 1) * CT], ALU.add).then_inc(acc_free, 1)
                for i in range(4 * SPC):
                    split_lo(ph["out"]["g0"] + i, i % RING)
                    if i % SPC == 1 and i > SPC:
                        residual(i // SPC - 1)
                residual(3)
                dve.wait_ge(acc_free, 2 + ph["out"]["a0"] + 4)
                normalise(2 * r + 1, x1, h2)
                leave(dve, "dve"); n += 1

                enter(dve, "dve", n)
                stream(ph["pq"])
                leave(dve, "dve"); n += 1

                enter(dve, "dve", n)
                own.after(dve, dve.memset(eidx[:, NT * SEL:], 0))
                for t in range(NT):
                    dve.wait_ge(s_out, 8 * r + 4 * t + 4)

                    def top16(values, val, idx, m):
                        for k in range(m):
                            ins = dve.max(val(k)[:, 0:8], values(k))
                        own.after(dve, ins)
                        for k in range(m):
                            dve.max_index(idx(k)[:, 0:8], val(k)[:, 0:8], values(k))
                        for k in range(m):
                            ins = dve.match_replace(values(k), val(k)[:, 0:8], values(k), LOWEST)
                        own.after(dve, ins)
                        for k in range(m):
                            ins = dve.max(val(k)[:, 8:16], values(k))
                        own.after(dve, ins)
                        for k in range(m):
                            ins = dve.max_index(idx(k)[:, 8:16], val(k)[:, 8:16], values(k))
                        own.after(dve, ins)

                    top16(lambda k: s[:, t, k, :], lambda k: topv[:, k, :], lambda k: topi[:, k, :], 2 * PH)
                    own.after(dve, dve.tensor_copy(topf[:, :, :], topi[:, :, :]))
                    pairs_v = topv[:, :, :].rearrange("p (h c) k -> p h c k", c=2)
                    own.after(dve, dve.tensor_tensor(
                        cand[:, :, :].rearrange("p h (a b) -> p h a b", a=TOPK),
                        pairs_v[:, :, 0, :].unsqueeze(3).to_broadcast([P, PH, TOPK, TOPK]),
                        pairs_v[:, :, 1, :].unsqueeze(2).to_broadcast([P, PH, TOPK, TOPK]), ALU.add))
                    top16(lambda k: cand[:, k, :], lambda k: cv[:, k, :], lambda k: ci[:, k, :], PH)
                    dve.tensor_tensor(gsel[:, t, :].rearrange("p (h k) -> p h k", h=PH), cv[:, :, :],
                                      cv[:, :, 0:1].to_broadcast([P, PH, TOPK]), ALU.subtract).then_inc(shifted, 1)
                    cflat = ci[:, :, :].rearrange("p h k -> p (h k)")
                    pairs_i = topf[:, :, :].rearrange("p (h c) k -> p h c k", c=2)
                    for c, e in ((0, e1), (1, e2)):
                        if c == 0:
                            own.after(dve, dve.tensor_scalar(cpart[:, :], cflat, 4, None, ALU.logical_shift_right))
                        else:
                            own.after(dve, dve.tensor_scalar(cpart[:, :], cflat, 15, None, ALU.bitwise_and))
                        own.after(dve, dve.tensor_copy(cpf[:, :], cpart[:, :]))
                        own.after(dve, dve.tensor_tensor(eq[:, :, :], cpf[:, :].unsqueeze(2).to_broadcast([P, SEL, TOPK]),
                                                         iota[:, :].unsqueeze(1).to_broadcast([P, SEL, TOPK]), ALU.is_equal))
                        eqh = eq[:, :, :].rearrange("p (h k) a -> p h k a", h=PH)
                        own.after(dve, dve.tensor_tensor(eqh, eqh, pairs_i[:, :, c, :].unsqueeze(2).to_broadcast([P, PH, TOPK, TOPK]),
                                                         ALU.mult))
                        own.after(dve, dve.tensor_reduce(e[:, :], eq[:, :, :], AX.X, ALU.add))
                    own.after(dve, dve.scalar_tensor_tensor(e1[:, :], e1[:, :], float(NKEYS), e2[:, :], ALU.mult, ALU.add))
                    own.after(dve, dve.tensor_copy(eidx[:, t * SEL:(t + 1) * SEL], e1[:, :]))
                    dve.wait_ge(exped, NT * r + t + 1)
                    gv = gsel[:, t, :].rearrange("p (h k) -> p h k", h=PH)
                    own.after(dve, dve.tensor_reduce(gsum[:, :], gv, AX.X, ALU.add))
                    own.after(dve, dve.reciprocal(gsum[:, :], gsum[:, :]))
                    own.after(dve, dve.tensor_tensor(gv, gv, gsum[:, :].unsqueeze(2).to_broadcast([P, PH, TOPK]), ALU.mult))
                leave(dve, "dve"); n += 1

                enter(dve, "dve", n)
                for table in range(2):
                    first = 2 * r + table
                    if table:
                        dve.wait_ge(gelu_done, r + 1)
                        own.after(dve, dve.tensor_tensor(coef[:, :, :], coef[:, :, :], gsel[:, :, :], ALU.mult))
                        dve.wait_ge(x1_back, 16 * (r + 1))
                    for half in range(2):
                        dve.tensor_copy(stage_i[:, 4 * half:4 * half + 4], eidx[:, 4 * half:4 * half + 4]).then_inc(idx_ready, 1)
                    for t in range(NT):
                        with dve.Fori(0, SEL // 8) as i:
                            before = first * NT * SEL + t * SEL
                            if table:
                                dve.tensor_copy(stage_d[:, :], coef[:, t, bass.ds(i * 8, 8)]).then_inc(row_used, 1)
                                dve.wait_ge(row_used, i + (before // 8 + 2))
                            else:
                                dve.wait_ge(row_used, i + (before // 8 + 1))
                            for half in range(2):
                                for j in range(4 * half, 4 * half + 4):
                                    dve.wait_ge(row_in[j], i * 16 + (before // 8 * 16 + 16))
                                    if table:
                                        ins = dve.scalar_tensor_tensor(acc[:, t, :], rows[:, j, :], stage_d[:, j:j + 1], acc[:, t, :],
                                                                       ALU.mult, ALU.add)
                                        ins.then_inc(summed, 1)
                                        dve.wait_ge(summed, i * 8 + ((NT * r + t) * SEL + j + 1))
                                    else:
                                        dve.wait_ge(dotted, i * 8 + ((NT * r + t) * SEL + j + 1))
                                        ins = dve.tensor_tensor_reduce(out=dump[:, j % 2, :], in0=rows[:, j, :], in1=h2[:, t, :],
                                                                       scale=1.0, scalar=0.0, op0=ALU.mult, op1=ALU.add,
                                                                       accum_out=stage_d[:, j:j + 1])
                                        ins.then_inc(dotted, 1)
                                if not table:
                                    dve.wait_ge(dotted, i * 8 + ((NT * r + t) * SEL + 4 * half + 4 + 2))
                                dve.wait_ge(ticked, i * 2 + (before // 4 + half + 1))
                                dve.tensor_copy(stage_i[:, 4 * half:4 * half + 4],
                                                eidx[:, bass.ds(i * 8 + (t * SEL + 8 + 4 * half), 4)]).then_inc(idx_ready, 1)
                            if not table:
                                dve.tensor_copy(dots[:, t, bass.ds(i * 8, 8)], stage_d[:, :]).then_inc(row_used, 1)
                    if not table:
                        dve.drain().then_inc(dots_done, 1)
                leave(dve, "dve"); n += 1

        @block.tensor
        def _(pe):
            pe.wait_ge(consts_in, 96)
            pe.sem_inc(slab_done, 2)
            pe.sem_inc(acc_free, 2)

            def slab(g_, j, ks, form, lhs, b0, first, last):
                hi, lo = lhs
                for part, (wt, other) in enumerate(((w_hi, hi), (w_hi, lo), (w_lo, hi))):
                    if part == 0:
                        pe.wait_ge(hi_ready, g_ + 1)
                    if part == 2:
                        pe.wait_ge(lo_ready, g_ + 1)
                    for kk in range(SK):
                        k = ks + kk
                        start = first and part == 0 and kk == 0
                        stop = last and part == 2 and kk == SK - 1
                        if form == "rows":
                            for t in range(NT):
                                ins = pe.matmul(ps[:, b0 + t, :], other[:, k, t * P:(t + 1) * P], wt[:, j % 2, kk, :],
                                                start=start, stop=stop)
                        else:
                            for q in range(4):
                                ins = pe.matmul(ps[:, b0 + q // 2, (q % 2) * TOK:(q % 2 + 1) * TOK],
                                                wt[:, j % 2, kk, q * P:(q + 1) * P], other[:, k, :],
                                                start=start and q % 2 == 0, stop=stop, skip_group_check=True)
                ins.then_inc(slab_done, 1)
                return ins

            def stream(ph, form):
                def pair(i):
                    for c in range(2):
                        pe.wait_ge(acc_free, i * 2 + (ph["a0"] + c + 1))
                        for j in range(SPC):
                            slab(i * (2 * SPC) + (ph["g0"] + SPC * c + j), j, SK * j, form, (ht_hi, ht_lo), 2 * c,
                                 j == 0, j == SPC - 1)
                with pe.Fori(0, ph["pairs"]) as i:
                    pair(i)

            def normalise(k, src):
                for t in range(NT):
                    pe.wait_ge(normed, k * NT + t + 1)
                    for q in range(4):
                        if t:
                            pe.wait_ge(turn_lo, k * 8 + q + 1)
                        for c in range(4):
                            ins = pe.transpose(ps[:, 4 + q, c * P:(c + 1) * P], src[:, t, (4 * q + c) * P:(4 * q + c + 1) * P], ident[:, :])
                        ins.then_inc(turned, 1)

            n = 0
            for r in range(REQ):
                ph = phases[r]
                enter(pe, "pe", n)
                normalise(2 * r, x1)
                leave(pe, "pe"); n += 1

                enter(pe, "pe", n)
                stream(ph["qkv"], "rows")
                leave(pe, "pe"); n += 1

                enter(pe, "pe", n)
                pe.wait_ge(roped, r + 1)
                for u, c in enumerate(QK_TILES):
                    nh = 4 if c < 11 else 2
                    if u >= 2:
                        pe.wait_ge(qk_out, 9 * r + u - 1)
                    b0 = 4 * (u % 2)
                    for h in range(nh):
                        for t in range(NT):
                            ins = pe.transpose(ps[:, b0 + h // 2, (h % 2) * TOK + t * P:(h % 2) * TOK + (t + 1) * P],
                                               raw[:, c, t, h * DH:(h + 1) * DH], ident[:, :])
                    ins.then_inc(qk_turned, 1)
                pe.wait_ge(qk_out, 9 * (r + 1))

                def scores(u):
                    uu = N_UNITS * r + u
                    b0 = 2 * (u % 2)
                    if u >= 2:
                        pe.wait_ge(exp_done, uu - 1)
                    if u < 8:
                        hh, t = u // 2, u % 2
                        for g_ in range(A_GROUPS):
                            qh = 4 * g_ + hh
                            ins = pe.matmul(ps[:, b0 + g_ // 2, (g_ % 2) * TOK:(g_ % 2 + 1) * TOK],
                                            qkt[:, qh, t * P:(t + 1) * P], qkt[:, 12 + qh, :], start=True, stop=True)
                    else:
                        qh = u - 8
                        for t in range(NT):
                            ins = pe.matmul(ps[:, b0, t * TOK:(t + 1) * TOK], qkt[:, 24 + qh, t * P:(t + 1) * P],
                                            qkt[:, 32 + qh // 4, :], start=True, stop=True)
                    ins.then_inc(sc_ready, 1)

                scores(0)
                for u in range(N_UNITS):
                    uu = N_UNITS * r + u
                    if u + 1 < N_UNITS:
                        scores(u + 1)
                    pe.wait_ge(p_ready, uu + 1)
                    if uu:
                        pe.wait_ge(pt_ready, uu)
                    if u < 8:
                        for k in range(6):
                            ins = pe.transpose(ps[:, 4 + k // 4, (k % 4) * P:(k % 4 + 1) * P],
                                               prob[:, u % 2, k * P:(k + 1) * P], ident[:, :])
                    else:
                        for t in range(NT):
                            for k in range(2):
                                ins = pe.transpose(ps[:, 4, k * TOK + t * P:k * TOK + (t + 1) * P],
                                                   prob[:, u % 2, t * TOK + k * P:t * TOK + (k + 1) * P], ident[:, :])
                    ins.then_inc(p_turned, 1)
                    if u >= 8 or u % 2 == 1:
                        o_ = out_of(u)
                        pe.wait_ge(pt_ready, uu + 1)
                        if o_ >= 2:
                            pe.wait_ge(o_lo, N_OUT * r + o_ - 1)
                        if u < 8:
                            vals = [raw[:, 6 + k // 2, k % 2, o_ * DH:(o_ + 1) * DH] for k in range(6)]
                        else:
                            kv = 256 + (u - 8) // 4 * DH
                            vals = [raw[:, 11, k, kv:kv + DH] for k in range(2)]
                        for k, val in enumerate(vals):
                            ins = pe.matmul(ps[:, 6 + o_ % 2, 0:TOK], val, pt[:, o_ % 2, k, :], start=(k == 0), stop=(k == len(vals) - 1))
                        ins.then_inc(pv_ready, 1)
                leave(pe, "pe"); n += 1

                enter(pe, "pe", n)
                stream(ph["gate"], "columns")
                leave(pe, "pe"); n += 1

                enter(pe, "pe", n)
                gg = ph["branch"]["g0"]
                for ct in range(4):
                    for side, (k0, ns) in enumerate(((0, 1), (4, 2))):
                        pe.wait_ge(acc_free, ph["branch"]["a0"] + 2 * ct + side + 1)
                        for j in range(ns):
                            slab(gg, gg, k0 + SK * j, "columns", (ot_hi, ot_lo), 2 * side, j == 0, j == ns - 1)
                            gg += 1
                leave(pe, "pe"); n += 1

                enter(pe, "pe", n)
                stream(ph["out"], "rows")
                normalise(2 * r + 1, h2)
                leave(pe, "pe"); n += 1

                enter(pe, "pe", n)
                stream(ph["pq"], "columns")
                pe.wait_ge(sk_in, 16 * (r + 1))
                for q in range(4):
                    for c in range(4):
                        ins = pe.transpose(ps[:, 4 + q, c * P:(c + 1) * P], skn[:, 4 * q + c, :], ident[:, :])
                    ins.then_inc(sk_turned, 1)
                leave(pe, "pe"); n += 1

                enter(pe, "pe", n)
                for q in range(8):
                    t, c = q // 4, q % 4
                    for k in range(4):
                        ins = pe.matmul(ps[:, q, k * P:(k + 1) * P], qt[:, 4 * c + k, t * P:(t + 1) * P], skt[:, 4 * c + k, :],
                                        start=True, stop=True)
                    ins.then_inc(s_ready, 1)
                leave(pe, "pe"); n += 1

                enter(pe, "pe", n)
                leave(pe, "pe"); n += 1


def kernel(**inputs):
    import concourse.bacc as bacc
    from concourse.bass_utils import run_bass_kernel_spmd as run

    f = lambda name: np.ascontiguousarray(inputs[name][0])
    rows = lambda v, n: np.ascontiguousarray(np.broadcast_to(v, (n,) + v.shape))
    q = np.arange(TOK)
    near = np.abs(q[:, None] - q[None, :])
    allowed = np.concatenate([near <= 64, near % 4 == 0, near % 16 == 0], axis=1)
    mask = np.where(allowed, 0.0, NEG).astype(np.float32).reshape(NT, P, A_GROUPS * TOK).transpose(1, 0, 2)

    def table(pos, dim, theta):
        inv = np.float32(theta) ** (-(np.arange(0, dim, 2, dtype=np.float32) / np.float32(dim)))
        ang = pos.astype(np.float32)[:, None] * inv[None, :].astype(np.float32)
        return np.stack([np.cos(ang), np.sin(ang)]).astype(np.float32)
    rope_a = table(q, 32, 500000.0).reshape(2, NT, P, ROT).transpose(2, 0, 1, 3)
    rope_b = np.stack([table(q // 64, 64, 10000.0), table(q % 64, 64, 10000.0)], axis=2).reshape(2, NT, P, 2, 32).transpose(2, 0, 1, 3, 4)
    gains = np.stack([f("qn_a"), f("kn_a"), f("qn_b"), f("kn_b")])
    arrays = {
        "x": np.concatenate([inputs["x_prompt"], inputs["x_sample"]], axis=0),
        "g_mix_b": rows(f("g_mix"), P), "g_ffn_b": rows(f("g_ffn"), P), "w_in": f("w_in"), "gains": rows(gains, P),
        "w_br_a": f("w_br_a"), "w_br_b": f("w_br_b"), "w_out": f("w_out"), "w_pq": f("w_pq"),
        "sub_keys": f("sub_keys").reshape(2 * PH, NKEYS, P), "u_emb": f("u_emb"), "v_emb": f("v_emb"),
        "ident_c": np.eye(P, dtype=np.float32), "mask_c": mask, "rope_a_c": rope_a, "rope_b_c": rope_b,
        "iota_c": rows(np.arange(TOPK, dtype=np.float32), P),
    }
    arrays = {k: np.ascontiguousarray(v) for k, v in arrays.items()}
    nc = bacc.Bacc("TRN2", target_bir_lowering=False, num_devices=1)
    args = [nc.dram_tensor(k, v.shape, F32, kind="ExternalInput").ap() for k, v in arrays.items()]
    y = nc.dram_tensor("y", (REQ, TOK, D), F32, kind="ExternalOutput").ap()
    encoder(nc, *args, y)
    out = run(nc, [arrays], core_ids=[0]).results[0]["y"]
    return out[0:1], out[1:2]
```

```python
import numpy as np
import concourse.bass as bass
from concourse import mybir

F32 = mybir.dt.float32
F32R = mybir.dt.float32r
U32 = mybir.dt.uint32
ALU = mybir.AluOpType
ACT = mybir.ActivationFunctionType
AX = mybir.AxisListType

P = 128
D = 2048
KC = D // P
TOK = 256
NT = TOK // P
REQ = 2
BR_A, BR_SLABS = 2, 6
DH = 128
SCALE = DH ** -0.5
EPS = 1e-6
CT = 512
SK = 2
SPC = KC // SK
RING = 4
ROWS = 4
A_HEADS, A_MERGED, A_GROUPS = 12, 4, 3
B_HEADS, B_KV = 8, 2
QKV_CT = 12
GATE_CT = 8
ROT = 16
PH, NKEYS, TOPK = 8, 128, 16
SEL = PH * TOPK
GROUPS = NT * SEL // 8
HALVES, HB = 2, NKEYS // 2
BODY = 8
NEG = -1.0e30
LOWEST = -3.0e38


TILE_ORDER = (0, 1, 2, 3, 4, 5, 9, 10, 11, 6, 7, 8)
N_QK = 9
N_UNITS = 16
N_OUT = 12


def out_of(u):
    return u // 2 if u < 8 else u - 4


class Counter:

    def __init__(self, sem):
        self.sem, self.n = sem, 0

    def after(self, eng, ins):
        self.n += 1
        ins.then_inc(self.sem, 1)
        eng.wait_ge(self.sem, self.n)


def encoder(nc, x, g_mix_b, g_ffn_b, w_in, gains, w_br_a, w_br_b, w_out, w_pq, sub_keys, u_emb, v_emb,
            ident_c, mask_c, rope_a_c, rope_b_c, iota_c, y):
    base = 16512
    place = {}

    def at(name, offset, shape, dtype):
        place[name] = nc.alloc_sbuf_tensor_at(name, [P] + shape, dtype, offset=offset)
        return place[name]

    o = base
    ident = at("ident", o, [P], F32); o += 512
    rope_a = at("rope_a", o, [2, NT, ROT], F32); o += 256
    rope_b = at("rope_b", o, [2, NT, 2, 32], F32); o += 1024
    gain = at("gain", o, [4, DH], F32); o += 2048
    mask = at("mask", o, [NT, A_GROUPS * TOK], F32)
    sel_t = at("sel_t", o, [3, TOK], F32); o += 6144
    iota = at("iota", o, [NKEYS], F32); o += 512
    tick = at("tick", o, [4], F32); o += 32
    stat = at("stat", o, [16], F32); o += 64
    eidx = at("eidx", o, [2 * NT * SEL + 8], U32); o += 2080
    gsel = [at(f"gsel{r}", o + 1024 * r, [NT, SEL], F32) for r in range(REQ)]; o += 2048
    zeros = at("zeros", o, [CT], mybir.dt.bfloat16); o += 1024
    dots = at("dots", o, [NT, SEL], F32); o += 1024
    coef = at("coef", o, [NT, SEL], F32); o += 1024
    stage_i = at("stage_i", o, [8], U32); o += 32
    stage_d = at("stage_d", o, [8], F32); o += 32
    R_HT = o; o += 32768
    R_RAW = o; o += 49152
    R_OT = o; o += 24576
    R_W = o; o += 16384
    R_SPLIT = o; o += 19968
    R_H2 = o; o += 16384
    R_ROWS = o; o += 32768

    ht_hi = at("ht_hi", R_HT, [KC, TOK], F32R)
    ht_lo = at("ht_lo", R_HT + 16384, [KC, TOK], F32R)
    raw = at("raw", R_RAW, [QKV_CT, NT, CT], F32)

    def qkt(head):
        if head < 32:
            return raw[:, head // 4, :, :].rearrange("p t c -> p (t c)")[:, head % 4 * TOK:(head % 4 + 1) * TOK]
        return raw[:, N_QK - 1, head - 32, 0:TOK]

    ot_hi = at("ot_hi", R_OT, [12, TOK], F32R)
    ot_lo = at("ot_lo", R_OT + 12288, [12, TOK], F32R)
    xin = at("xin", R_RAW, [NT, D], F32)
    x1 = at("x1", R_RAW + 16384, [NT, D], F32)
    gvec = at("gvec", R_RAW + 32768, [D], F32)
    junk = at("junk", R_RAW + 40960, [D], F32)
    sg = at("sg", R_RAW, [2 * KC, TOK], F32)
    m1 = at("m1", R_RAW + 32768, [4, TOK], F32)
    m2 = at("m2", R_RAW + 36864, [4, TOK], F32)
    skn = at("skn", R_RAW, [2 * PH, P], F32)
    skt = at("skt", R_RAW + 8192, [2 * PH, P], F32)
    qt = at("qt", R_RAW + 16384, [2 * PH, TOK], F32)
    w = at("w", R_W, [RING, SK, CT], F32)
    w_hi = at("w_hi", R_SPLIT, [2, SK, CT], F32R)
    w_lo = at("w_lo", R_SPLIT + 8192, [2, SK, CT], F32R)
    h2 = [at("h2_0", R_H2, [NT, D], F32), at("h2_1", R_OT, [NT, D], F32)]
    prob = at("prob", R_SPLIT, [2, A_GROUPS * TOK], F32)
    pt = at("pt", R_SPLIT + 6144, [2, 6, TOK], F32)
    sq = at("sq", R_SPLIT, [2 * CT], F32)
    rt = at("rt", R_SPLIT + 4096, [4, 384], F32)
    ss = at("ss", R_SPLIT + 18432, [72], F32)
    rs = at("rs", R_SPLIT + 18720, [72], F32)
    rtmp = at("rtmp", R_SPLIT + 19008, [72], F32)
    ust = at("ust", R_SPLIT + 19296, [N_UNITS, 8], F32)
    s = at("s", R_OT, [NT, 2 * PH, NKEYS], F32)
    cand = at("cand", R_SPLIT, [PH, TOPK * TOPK], F32)
    eq = at("eq", R_OT + 16384, [PH * TOPK, TOPK], F32)
    topv = at("topv", R_RAW + 32768, [2 * PH, TOPK], F32)
    topi = at("topi", R_RAW + 33792, [2 * PH, TOPK], U32)
    topf = at("topf", R_RAW + 34816, [2 * PH, TOPK], F32)
    cv = at("cv", R_RAW + 35840, [PH, TOPK], F32)
    ci = at("ci", R_RAW + 36352, [PH, TOPK], U32)
    cpart = at("cpart", R_RAW + 36864, [SEL], U32)
    cpf = at("cpf", R_RAW + 37376, [SEL], F32)
    keys = at("keys", R_RAW + 37888, [2, NT, SEL], F32)
    esum = at("esum", R_RAW + 39936, [SEL], F32)
    gsum = at("gsum", R_RAW + 40448, [PH], F32)
    rows = at("rows", R_ROWS, [ROWS, D], F32)
    acc = at("acc", R_H2, [NT, D], F32)
    coefs = at("coefs", R_RAW, [HB, TOK], F32)
    c_hi = at("c_hi", R_RAW + 65536, [2, TOK], F32R)
    c_lo = at("c_lo", R_RAW + 67584, [2, TOK], F32R)
    ge = at("ge", R_RAW + 69632, [2, TOK], F32)
    total = at("total", R_RAW, [NT, D], F32)
    pick1 = at("pick1", R_SPLIT, [2, 8, HB], F32)
    pick2 = at("pick2", R_SPLIT + 4096, [2, 8, NKEYS], F32)

    ps = nc.alloc_psum_tensor("ps", [P, 8, 512], F32)
    S = nc.alloc_semaphore
    consts_in = S("consts_in")
    x_in, g_in, xres_in, g2_in, sk_in, y_out, x1_back = (S(n) for n in ("x_in", "g_in", "xres_in", "g2_in", "sk_in", "y_out", "x1_back"))
    w_loaded = [S(f"w_loaded{j}") for j in range(RING)]
    hi_ready, lo_ready, slab_done = S("hi_ready"), S("lo_ready"), S("slab_done")
    acc_free = S("acc_free")
    done = {n: S(f"done_{n}") for n in ("pe", "act", "dve")}
    act_own, dve_own = S("act_own"), S("dve_own")
    used, copied, staged = S("used"), S("copied"), S("staged")
    ticked, acc_done, x1_in1 = S("ticked"), S("acc_done"), S("x1_in1")
    zero_ready, sel_ready, sel_turned, sel_out = S("zero_ready"), S("sel_ready"), S("sel_turned"), S("sel_out")
    picks_free = S("picks_free")
    picks_ready, spread = S("picks_ready"), S("spread")
    u_turned, a_free, c_made, c_hi_ready, c_lo_ready, total_done, y_half = (
        S(n) for n in ("u_turned", "a_free", "c_made", "c_hi_ready", "c_lo_ready", "total_done", "y_half"))
    sum_ready, mean_ready, root_ready = S("sum_ready"), S("mean_ready"), S("root_ready")
    normed, turned, turn_hi, turn_lo = S("normed"), S("turned"), S("turn_hi"), S("turn_lo")
    squared, sq_free, roped, qk_turned, qk_out = S("squared"), S("sq_free"), S("roped"), S("qk_turned"), S("qk_out")
    sc_ready, sc_max, exp_done, p_ready, p_turned, pt_ready, pv_ready, o_hi, o_lo = (
        S(n) for n in ("sc_ready", "sc_max", "exp_done", "p_ready", "p_turned", "pt_ready", "pv_ready", "o_hi", "o_lo"))
    merged, merged_hi = S("merged"), S("merged_hi")
    sk_turned, sk_out, s_ready, s_out, shifted, exped = (S(n) for n in ("sk_turned", "sk_out", "s_ready", "s_out", "shifted", "exped"))
    row_in = [S(f"row_in{j}") for j in range(ROWS)]
    dots_done, gelu_done = S("dots_done"), S("gelu_done")

    def slabs(columns, slab_base, acc_base):
        return dict(pairs=columns // 2, g0=slab_base, a0=acc_base)

    phases, g, a = [], 0, 0
    for r in range(REQ):
        ph = {}
        for name, n in (("qkv", QKV_CT), ("gate", GATE_CT)):
            ph[name] = slabs(n, g, a); g += SPC * n; a += n
        ph["branch"] = dict(g0=g, a0=a); g += 4 * BR_SLABS; a += 8
        for name, n in (("out", 4), ("pq", 4)):
            ph[name] = slabs(n, g, a); g += SPC * n; a += n
        phases.append(ph)
    table_g0 = [[g + 4 * HB * h, g + 4 * HB * h + 2 * HB] for h in range(HALVES)]

    w_view = {
        "qkv": (w_in.rearrange("(s k p) n -> s p k n", k=SK, p=P), 0),
        "gate": (w_in.rearrange("(s k p) n -> s p k n", k=SK, p=P), QKV_CT * CT),
        "out": (w_out.rearrange("(s k p) n -> s p k n", k=SK, p=P), 0),
        "pq": (w_pq.rearrange("(s k p) n -> s p k n", k=SK, p=P), 0),
    }
    bra = w_br_a.rearrange("(s k p) n -> s p k n", k=SK, p=P)
    brb = w_br_b.rearrange("(s k p) n -> s p k n", k=SK, p=P)

    def enter(eng, me, n):
        for other in done:
            if other != me and n:
                eng.wait_ge(done[other], n)

    def leave(eng, me):
        eng.drain().then_inc(done[me], 1)

    block_cm = nc.Block()
    with block_cm as block:

        @block.sync
        def _(sp):
            def load(src, slot, g_):
                if not isinstance(g_, int) or g_ >= RING:
                    sp.wait_ge(lo_ready, g_ - RING + 1)
                sp.dma_start(w[:, slot, :, :], src).then_inc(w_loaded[slot], 16)

            def stream(name, ph):
                view, col0 = w_view[name]

                def pair(i, tiles=None):
                    for c in range(2):
                        for j in range(SPC):
                            g_ = i * (2 * SPC) + (ph["g0"] + SPC * c + j)
                            n0 = i * (2 * CT) + (col0 + c * CT) if tiles is None else tiles[c] * CT
                            load(view[j, :, :, bass.ds(n0, CT)], j % RING, g_)
                pair(0)
                with sp.Fori(1, 3 if name == "qkv" else ph["pairs"]) as i:
                    pair(i)
                if name == "qkv":
                    for i in range(3, 6):
                        pair(i, TILE_ORDER[2 * i:2 * i + 2])

            for r in range(REQ):
                ph = phases[r]
                stream("qkv", ph["qkv"])
                stream("gate", ph["gate"])
                n = ph["branch"]["g0"]
                for ct in range(4):
                    for src in [bra[k] for k in range(BR_A)] + [brb[k] for k in range(BR_SLABS - BR_A)]:
                        load(src[:, :, ct * CT:(ct + 1) * CT], n % RING, n)
                        n += 1
                stream("out", ph["out"])
                stream("pq", ph["pq"])
            for h in range(HALVES):
                for table, emb in enumerate((u_emb, v_emb)):
                    blocks = emb.rearrange("(b p) d -> p b d", p=P)
                    with sp.Fori(0, HB // BODY) as i:
                        for j in range(2 * BODY):
                            sp.wait_ge(lo_ready, i * (2 * BODY) + (table_g0[h][table] + j - RING + 1))
                            sp.dma_start(w[:, j % RING, :, :].rearrange("p k c -> p (k c)").unsqueeze(1),
                                         blocks[:, bass.ds(i * BODY + (HB * h + j // 2), 1), D // 2 * (j % 2):D // 2 * (j % 2 + 1)]
                                         ).then_inc(w_loaded[j % RING], 16)

        @block.gpsimd
        def _(pool):
            pool.wait_ge(consts_in, 96)
            pool.wait_ge(staged, 1)
            for table, emb in enumerate((u_emb, v_emb)):
                with pool.Fori(0, GROUPS) as i:
                    for j in range(0, 8, 2):
                        pool.wait_ge(used, i * 8 + (8 * GROUPS * table + j + 2))
                        pool.tensor_tensor(tick[:, j // 2:j // 2 + 1], iota[:, 0:1], iota[:, 0:1], ALU.add).then_inc(ticked, 1)
                        for jj in (j, j + 1):
                            pool.indirect_dma_start(rows[:, jj % ROWS, :], None, emb,
                                                    bass.IndirectOffsetOnAxis(ap=stage_i[:, jj:jj + 1], axis=0)).then_inc(row_in[jj % ROWS], 16)

        @block.scalar
        def _(act):
            for dst, src in ((ident[:, :], ident_c), (rope_a[:, :, :, :], rope_a_c), (rope_b[:, :, :, :, :], rope_b_c),
                             (gain[:, :, :], gains), (mask[:, :, :], mask_c), (iota[:, :], iota_c)):
                act.dma_start(dst, src).then_inc(consts_in, 16)

            def split_hi(g_, j):
                act.wait_ge(w_loaded[j % RING], loads(g_, j))
                act.wait_ge(slab_done, g_ + 1)
                act.activation(w_hi[:, j % 2, :, :], w[:, j % RING, :, :], ACT.Copy).then_inc(hi_ready, 1)

            def loads(g_, j):
                return (g_ - (j % RING)) * (16 // RING) + 16

            def stream(ph, evacuate):
                def pair(i, first=False):
                    for c in range(2):
                        for j in range(SPC):
                            split_hi(i * (2 * SPC) + (ph["g0"] + SPC * c + j), j)
                            if j == 3 and not (first and c == 0):
                                out(i * 2 + (c - 1), 1 - c)

                def out(ct, side):
                    act.wait_ge(slab_done, ct * SPC + (ph["g0"] + SPC + 2))
                    evacuate(ct, side).then_inc(acc_free, 1)
                pair(0, True)
                with act.Fori(1, ph["pairs"]) as i:
                    pair(i)
                out(2 * ph["pairs"] - 1, 1)

            def normalise(k, m_):
                for t in range(NT):
                    if t:
                        act.wait_ge(sum_ready, NT * k + t)
                    act.activation(junk[:, :], (xin if k % 2 == 0 else x1)[:, t, :], ACT.Square,
                                   accum_out=stat[:, t:t + 1]).then_inc(sum_ready, 1)
                act.wait_ge(mean_ready, m_ + 1)
                act.activation(stat[:, 4:6], stat[:, 2:4], ACT.Sqrt).then_inc(root_ready, 1)
                for t in range(NT):
                    for q in range(4):
                        m = k * 8 + t * 4 + q
                        act.wait_ge(turned, m + 1)
                        act.activation(ht_hi[:, 4 * q:4 * q + 4, t * P:(t + 1) * P],
                                       ps[:, 4 + q, :].rearrange("p (k t) -> p k t", k=4), ACT.Copy).then_inc(turn_hi, 1)

            n = 0
            for r in range(REQ):
                ph = phases[r]
                xr = x[r].rearrange("(t p) d -> p t d", p=P)
                yr = y[r].rearrange("(t p) d -> p t d", p=P)
                enter(act, "act", n)
                act.dma_start(xin[:, :, :], xr).then_inc(x_in, 16)
                act.dma_start(gvec[:, :], g_mix_b).then_inc(g_in, 16)
                act.wait_ge(x_in, 16 * (r + 1))
                normalise(2 * r, 3 * r)
                leave(act, "act"); n += 1

                enter(act, "act", n)
                stream(ph["qkv"], lambda ct, side: act.activation(
                    raw[:, bass.ds(ct, 1), :, :].rearrange("p a t c -> p (a t c)"),
                    ps[:, 2 * side:2 * side + 2, :].rearrange("p b c -> p (b c)"), ACT.Copy))
                leave(act, "act"); n += 1

                enter(act, "act", n)
                for u in range(N_QK):
                    wid = CT if u < 8 else 256
                    if u:
                        act.wait_ge(sq_free, 9 * r + u)
                    act.activation(sq[:, 0:2 * wid].rearrange("p (t c) -> p t c", t=2), raw[:, u, :, 0:wid],
                                   ACT.Square).then_inc(squared, 1)
                act.wait_ge(mean_ready, 3 * r + 2)
                act.activation(rs[:, 0:68], ss[:, 0:68], ACT.Sqrt).then_inc(root_ready, 1)
                for u in range(N_QK):
                    act.wait_ge(qk_turned, 9 * r + u + 1)
                    b0 = 4 * (u % 2)
                    if u < 8:
                        act.activation(raw[:, u, :, :], ps[:, b0:b0 + 2, :], ACT.Copy).then_inc(qk_out, 1)
                    else:
                        act.activation(raw[:, u, :, 0:TOK], ps[:, b0, :].rearrange("p (h t) -> p h t", h=2),
                                       ACT.Copy).then_inc(qk_out, 1)
                for u in range(N_UNITS):
                    uu = N_UNITS * r + u
                    act.wait_ge(sc_max, uu + 1)
                    if u < 8:
                        act.activation(prob[:, u % 2, :], prob[:, u % 2, :], ACT.Exp, bias=ust[:, u, 2:3], scale=SCALE,
                                       accum_out=ust[:, u, 4:5]).then_inc(exp_done, 1)
                    else:
                        b0 = 2 * (u % 2)
                        for t in range(NT):
                            ins = act.activation(prob[:, u % 2, t * TOK:(t + 1) * TOK], ps[:, b0, t * TOK:(t + 1) * TOK],
                                                 ACT.Exp, bias=ust[:, u, 2 + t:3 + t], scale=SCALE,
                                                 accum_out=ust[:, u, 4 + t:5 + t])
                        ins.then_inc(exp_done, 1)
                    act.wait_ge(p_turned, uu + 1)
                    o_, oi = out_of(u), N_OUT * r + out_of(u)
                    t = u % 2
                    if o_ >= 2 and (u >= 8 or t == 0):
                        act.wait_ge(pv_ready, oi - 1)
                    if u < 8:
                        act.activation(pt[:, o_ % 2, :, t * P:(t + 1) * P],
                                       ps[:, 4:6, :].rearrange("p b c -> p (b c)")[:, 0:768].rearrange("p (k q) -> p k q", k=6),
                                       ACT.Copy).then_inc(pt_ready, 1)
                    else:
                        act.activation(pt[:, o_ % 2, 0:2, :], ps[:, 4, :].rearrange("p (k q) -> p k q", k=2),
                                       ACT.Copy).then_inc(pt_ready, 1)
                    if u >= 8 or t == 1:
                        act.wait_ge(pv_ready, oi + 1)
                        act.activation(ot_hi[:, o_, :], ps[:, 6 + o_ % 2, 0:TOK], ACT.Copy).then_inc(o_hi, 1)
                leave(act, "act"); n += 1

                enter(act, "act", n)
                stream(ph["gate"], lambda ct, side: act.activation(
                    sg[:, bass.ds(ct * 4, 4), :].rearrange("p a t -> p (a t)"),
                    ps[:, 2 * side:2 * side + 2, :].rearrange("p b c -> p (b c)"), ACT.Sigmoid))
                leave(act, "act"); n += 1

                enter(act, "act", n)
                for ct in range(4):
                    for k in range(BR_SLABS):
                        gg = ph["branch"]["g0"] + BR_SLABS * ct + k
                        split_hi(gg, gg % RING)
                    act.wait_ge(merged, 4 * r + ct + 1)
                    act.activation(ht_hi[:, 4 * ct:4 * ct + 4, :], m1[:, :, :], ACT.Copy).then_inc(merged_hi, 1)
                leave(act, "act"); n += 1

                enter(act, "act", n)
                act.dma_start(xin[:, :, :], xr).then_inc(xres_in, 16)
                act.dma_start(gvec[:, :], g_ffn_b).then_inc(g2_in, 16)
                for i in range(2 * ph["out"]["pairs"] * SPC):
                    split_hi(ph["out"]["g0"] + i, i % RING)
                act.wait_ge(acc_free, 2 + ph["out"]["a0"] + 4)
                normalise(2 * r + 1, 3 * r + 2)
                leave(act, "act"); n += 1

                enter(act, "act", n)
                act.dma_start(yr, x1[:, :, :]).then_inc(y_out, 16)
                act.dma_start(skn[:, :, :], sub_keys.rearrange("c n d -> n c d")).then_inc(sk_in, 16)
                for i in range(2 * ph["pq"]["pairs"] * SPC):
                    split_hi(ph["pq"]["g0"] + i, i % RING)
                    if i % SPC == 3 and i > SPC:
                        ct = i // SPC - 1
                        if ct == 0:
                            act.wait_ge(y_out, 16 * (r + 1))
                        act.wait_ge(slab_done, ph["pq"]["g0"] + SPC * (ct + 1) + 2)
                        act.activation(qt[:, 4 * ct:4 * ct + 4, :].rearrange("p a t -> p (a t)"),
                                       ps[:, 2 * (ct % 2):2 * (ct % 2) + 2, :].rearrange("p b c -> p (b c)"),
                                       ACT.Copy).then_inc(acc_free, 1)
                act.wait_ge(slab_done, ph["pq"]["g0"] + SPC * 4 + 2)
                act.activation(qt[:, 12:16, :].rearrange("p a t -> p (a t)"),
                               ps[:, 2:4, :].rearrange("p b c -> p (b c)"), ACT.Copy).then_inc(acc_free, 1)
                for q in range(4):
                    act.wait_ge(sk_turned, 4 * r + q + 1)
                    act.activation(skt[:, 4 * q:4 * q + 4, :].rearrange("p a n -> p (a n)"), ps[:, 4 + q, :],
                                   ACT.Copy).then_inc(sk_out, 1)
                leave(act, "act"); n += 1

                enter(act, "act", n)
                for q in range(8):
                    act.wait_ge(s_ready, 8 * r + q + 1)
                    t, c = q // 4, q % 4
                    act.activation(s[:, t, 4 * c:4 * c + 4, :].rearrange("p a n -> p (a n)"), ps[:, q, :],
                                   ACT.Copy).then_inc(s_out, 1)
                for t in range(NT):
                    act.wait_ge(shifted, NT * r + t + 1)
                    act.activation(gsel[r][:, t, :], gsel[r][:, t, :], ACT.Exp).then_inc(exped, 1)
                if r == 1:
                    act.wait_ge(sel_turned, 1)
                    act.activation(sel_t[:, 0:2, :].rearrange("p a t -> p (a t)"), ps[:, 0, :], ACT.Copy)
                    act.activation(sel_t[:, 2, :], ps[:, 1, 0:TOK], ACT.Copy)
                leave(act, "act"); n += 1

            yr = [y[r].rearrange("(t p) d -> p t d", p=P) for r in range(REQ)]
            for h in range(HALVES):
                enter(act, "act", n)
                if h == 0:
                    act.wait_ge(dots_done, 1)
                    act.activation(coef[:, :, :], dots[:, :, :], ACT.Gelu).then_inc(gelu_done, 1)
                    act.dma_start(acc[:, :, :], yr[0]).then_inc(x1_back, 16)
                else:
                    act.wait_ge(y_half, 16)
                with act.Fori(0, TOK // 16) as i:
                    for c in range(2):
                        act.wait_ge(picks_free, i * 2 + (TOK // 8 * h + c + 3))
                        act.activation(coefs[:, :, bass.ds(i * 16 + 8 * c, 8)],
                                       ps[:, c, :].rearrange("p (m k) -> p k m", m=8), ACT.Copy).then_inc(spread, 1)
                leave(act, "act"); n += 1

                enter(act, "act", n)
                g0 = table_g0[h][0]

                def activate(b, par):
                    act.wait_ge(slab_done, b * 2 + (g0 + 2 + 2))
                    act.wait_ge(c_made, b + (HB * h + 1))
                    act.activation(ge[:, par, :], ps[:, 4 + par, 0:TOK], ACT.Gelu).then_inc(a_free, 1)

                def blocks(i, first=False):
                    for j in range(2 * BODY):
                        act.wait_ge(u_turned, i * (2 * BODY) + (2 * HB * h + j + 1))
                        act.wait_ge(slab_done, i * (2 * BODY) + (g0 + j + 1))
                        act.activation(w_hi[:, j % 2, :, :], ps[:, 2 * (j % 2):2 * (j % 2) + 2, :], ACT.Copy).then_inc(hi_ready, 1)
                        if j % 2 == 0 and not (first and j == 0):
                            activate(i * BODY + (j // 2 - 1), (j // 2 - 1) % 2)
                blocks(0, True)
                with act.Fori(1, HB // BODY) as i:
                    blocks(i)
                activate(HB - 1, 1)
                leave(act, "act"); n += 1

                enter(act, "act", n)
                g0 = table_g0[h][1]
                with act.Fori(0, HB // BODY) as i:
                    for j in range(2 * BODY):
                        split_hi(i * (2 * BODY) + (g0 + j), j)
                        if j % 2 == 0:
                            act.activation(c_hi[:, j // 2 % 2, :],
                                           coefs[:, bass.ds(i * BODY + j // 2, 1), :].rearrange("p a t -> p (a t)"),
                                           ACT.Copy).then_inc(c_hi_ready, 1)
                leave(act, "act"); n += 1

                enter(act, "act", n)
                act.dma_start(total[:, :, :], yr[1]).then_inc(x1_in1, 16)
                act.wait_ge(total_done, h + 1)
                act.dma_start(yr[1], total[:, :, :]).then_inc(y_half, 16)
                leave(act, "act"); n += 1
            act.wait_ge(acc_done, 1)
            act.dma_start(yr[0], acc[:, :, :]).then_inc(y_out, 16)
            act.wait_ge(y_out, 16 * (REQ + 1))
            act.wait_ge(y_half, 16 * HALVES)

        @block.vector
        def _(dve):
            own = Counter(dve_own)
            dve.sem_inc(used, ROWS)
            dve.sem_inc(copied, 1)
            dve.memset(zeros[:, :], 0.0).then_inc(zero_ready, 1)

            def split_lo(g_, j):
                dve.wait_ge(hi_ready, g_ + 1)
                dve.tensor_tensor(w_lo[:, j % 2, :, :], w[:, j % RING, :, :], w_hi[:, j % 2, :, :].bitcast(F32),
                                  ALU.subtract).then_inc(lo_ready, 1)

            def turn(K, j, table, t):
                first = table
                n_ = K * 8 + (8 * GROUPS * first + j)
                if j == 0:
                    dve.wait_ge(copied, K + (GROUPS * first + 1))
                    if table:
                        dve.wait_ge(used, n_ + ROWS)
                        dve.tensor_copy(stage_d[:, :], coef[:, :, :].rearrange("p t k -> p (t k)")[:, bass.ds(K * 8, 8)]).then_inc(copied, 1)
                        dve.wait_ge(copied, K + (GROUPS * first + 2))
                row = rows[:, j % ROWS, :]
                dve.wait_ge(row_in[j % ROWS], K * (16 * 8 // ROWS) + (16 * 8 // ROWS * GROUPS * first + 16 * (j // ROWS + 1)))
                if table == 0:
                    dve.tensor_tensor_reduce(out=row, in0=row, in1=h2[0][:, t, :], scale=1.0, scalar=0.0, op0=ALU.mult,
                                             op1=ALU.add, accum_out=stage_d[:, j:j + 1]).then_inc(used, 1)
                else:
                    dve.wait_ge(used, n_ + ROWS)
                    dve.scalar_tensor_tensor(acc[:, t, :], row, stage_d[:, j:j + 1], acc[:, t, :],
                                             ALU.mult, ALU.add).then_inc(used, 1)
                if j in (3, 7):
                    h = j // 4
                    dve.wait_ge(ticked, K * 4 + (4 * GROUPS * first + 2 * h + 2))
                    dve.tensor_copy(stage_i[:, 4 * h:4 * h + 4],
                                    eidx[:, bass.ds(K * 8 + (8 * GROUPS * table + 8 + 4 * h), 4)])
                if j == 7 and table == 0:
                    dve.wait_ge(used, n_ + ROWS + 1)
                    dve.tensor_copy(dots[:, :, :].rearrange("p t k -> p (t k)")[:, bass.ds(K * 8, 8)], stage_d[:, :]).then_inc(copied, 1)

            taken = [0]

            def turns(r, m):
                if r == 1:
                    for _ in range(m):
                        turn(taken[0] // 8, taken[0] % 8, 0, taken[0] // SEL)
                        taken[0] += 1

            def stream(ph, r):
                k0 = taken[0] // 8
                with dve.Fori(0, ph["pairs"]) as i:
                    for j in range(2 * SPC):
                        split_lo(i * (2 * SPC) + (ph["g0"] + j), j)
                        if r == 1 and j % 2:
                            turn(i + k0, j // 2, 0, 8 * k0 // SEL)
                if r == 1:
                    taken[0] += 8 * ph["pairs"]

            def inverse_root(mean, root, out, tmp):
                own.after(dve, dve.reciprocal(out, root))
                own.after(dve, dve.tensor_tensor(tmp, out, out, ALU.mult))
                own.after(dve, dve.tensor_tensor(tmp, tmp, mean, ALU.mult))
                own.after(dve, dve.tensor_scalar(tmp, tmp, -0.5, 1.5, ALU.mult, ALU.add))
                own.after(dve, dve.tensor_tensor(out, out, tmp, ALU.mult))

            def normalise(k, src, dst):
                dve.wait_ge(sum_ready, NT * (k + 1))
                dve.tensor_scalar(stat[:, 2:4], stat[:, 0:2], 1.0 / D, EPS, ALU.mult, ALU.add).then_inc(mean_ready, 1)
                dve.wait_ge(mean_ready, mean_count[0] + 1); mean_count[0] += 1
                dve.wait_ge(root_ready, root_count[0] + 1); root_count[0] += 1
                inverse_root(stat[:, 2:4], stat[:, 4:6], stat[:, 6:8], stat[:, 8:10])
                for t in range(NT):
                    dve.scalar_tensor_tensor(dst[:, t, :], src[:, t, :], stat[:, 6 + t:7 + t], gvec[:, :],
                                             ALU.mult, ALU.mult).then_inc(normed, 1)
                for t in range(NT):
                    for q in range(4):
                        dve.wait_ge(turn_hi, k * 8 + t * 4 + q + 1)
                        dve.tensor_tensor(ht_lo[:, 4 * q:4 * q + 4, t * P:(t + 1) * P],
                                          ps[:, 4 + q, :].rearrange("p (k t) -> p k t", k=4),
                                          ht_hi[:, 4 * q:4 * q + 4, t * P:(t + 1) * P].bitcast(F32),
                                          ALU.subtract).then_inc(turn_lo, 1)

            mean_count, root_count = [0], [0]
            n = 0
            dve.wait_ge(consts_in, 96)
            for r in range(REQ):
                ph = phases[r]
                enter(dve, "dve", n)
                dve.wait_ge(g_in, 16 * (r + 1))
                normalise(2 * r, xin, x1)
                leave(dve, "dve"); n += 1

                enter(dve, "dve", n)
                stream(ph["qkv"], r)
                leave(dve, "dve"); n += 1

                enter(dve, "dve", n)
                for u in range(N_QK):
                    nh = 8 if u < 8 else 4
                    dve.wait_ge(squared, 9 * r + u + 1)
                    dve.tensor_reduce(ss[:, 8 * u:8 * u + nh], sq[:, 0:nh * DH].rearrange("p (h d) -> p h d", d=DH),
                                      AX.X, ALU.add).then_inc(sq_free, 1)
                dve.wait_ge(sq_free, 9 * (r + 1))
                dve.tensor_scalar(ss[:, 0:68], ss[:, 0:68], 1.0 / DH, EPS, ALU.mult, ALU.add).then_inc(mean_ready, 1)
                dve.wait_ge(mean_ready, mean_count[0] + 1); mean_count[0] += 1
                dve.wait_ge(root_ready, root_count[0] + 1); root_count[0] += 1
                own.after(dve, dve.tensor_copy(rtmp[:, 0:68], rs[:, 0:68]))
                own.after(dve, dve.reciprocal(rs[:, 0:68], rtmp[:, 0:68]))
                own.after(dve, dve.tensor_tensor(rtmp[:, 0:68], rs[:, 0:68], rs[:, 0:68], ALU.mult))
                own.after(dve, dve.tensor_tensor(rtmp[:, 0:68], rtmp[:, 0:68], ss[:, 0:68], ALU.mult))
                own.after(dve, dve.tensor_scalar(rtmp[:, 0:68], rtmp[:, 0:68], -0.5, 1.5, ALU.mult, ALU.add))
                own.after(dve, dve.tensor_tensor(rs[:, 0:68], rs[:, 0:68], rtmp[:, 0:68], ALU.mult))
                turns(r, 4)
                for u in range(N_QK):
                    nh = 4 if u < 8 else 2
                    gi = 0 if u < 3 else 1 if u < 6 else 2 if u < 8 else 3
                    for t in range(NT):
                        for h in range(nh):
                            v = raw[:, u, t, h * DH:(h + 1) * DH]
                            i = 8 * u + nh * t + h
                            ins = dve.scalar_tensor_tensor(v, v, rs[:, i:i + 1], gain[:, gi, :], ALU.mult, ALU.mult)
                    turns(r, 1 if u < 8 else 0)
                own.after(dve, ins)

                def rotate(first, second, cos, sin, tmp):
                    dve.tensor_tensor(tmp(0), first, cos, ALU.mult)
                    dve.tensor_tensor(tmp(1), second, sin, ALU.mult)
                    dve.tensor_tensor(tmp(2), second, cos, ALU.mult)
                    own.after(dve, dve.tensor_tensor(tmp(3), first, sin, ALU.mult))
                    dve.tensor_tensor(first, tmp(0), tmp(1), ALU.subtract)
                    ins = dve.tensor_tensor(second, tmp(2), tmp(3), ALU.add)
                    own.after(dve, ins)

                for t in range(NT):
                    v = raw[:, 0:6, t, :].rearrange("p c (h d) -> p c h d", d=DH)
                    cs = [rope_a[:, k, t, :].unsqueeze(1).unsqueeze(1).to_broadcast([P, 6, 4, ROT]) for k in range(2)]
                    rotate(v[:, :, :, 0:ROT], v[:, :, :, ROT:2 * ROT], cs[0], cs[1],
                           lambda k: rt[:, k, :].rearrange("p (c h d) -> p c h d", c=6, d=ROT))
                turns(r, 2)
                for u in (6, 7, 8):
                    nh = 4 if u < 8 else 2
                    for t in range(NT):
                        v = raw[:, u, t, 0:nh * DH].rearrange("p (h s d) -> p h s d", s=2, d=64)
                        cs = [rope_b[:, k, t, :, :].unsqueeze(1).to_broadcast([P, nh, 2, 32]) for k in range(2)]
                        rotate(v[:, :, :, 0:32], v[:, :, :, 32:64], cs[0], cs[1],
                               lambda k: rt[:, k, 0:nh * 64].rearrange("p (h s d) -> p h s d", s=2, d=32))
                    turns(r, 0 if u == 8 else 1)
                dve.drain().then_inc(roped, 1)
                for u in range(N_UNITS):
                    uu = N_UNITS * r + u
                    turns(r, 4)
                    dve.wait_ge(sc_ready, uu + 1)
                    b0 = 2 * (u % 2)
                    if uu >= 2:
                        dve.wait_ge(p_turned, uu - 1)
                    if u < 8:
                        t = u % 2
                        own.after(dve, dve.tensor_tensor_reduce(
                            out=prob[:, u % 2, :], in0=ps[:, b0:b0 + 2, :].rearrange("p b c -> p (b c)")[:, 0:768],
                            in1=mask[:, t, :], scale=1.0, scalar=LOWEST, op0=ALU.add, op1=ALU.max, accum_out=ust[:, u, 0:1]))
                        dve.tensor_scalar(ust[:, u, 2:3], ust[:, u, 0:1], -SCALE, None, ALU.mult).then_inc(sc_max, 1)
                        dve.wait_ge(exp_done, uu + 1)
                        own.after(dve, dve.reciprocal(ust[:, u, 6:7], ust[:, u, 4:5]))
                        dve.tensor_scalar(prob[:, u % 2, :], prob[:, u % 2, :], ust[:, u, 6:7], None, ALU.mult).then_inc(p_ready, 1)
                    else:
                        own.after(dve, dve.tensor_reduce(ust[:, u, 0:2], ps[:, b0, :].rearrange("p (t k) -> p t k", t=NT), AX.X, ALU.max))
                        dve.tensor_scalar(ust[:, u, 2:4], ust[:, u, 0:2], -SCALE, None, ALU.mult).then_inc(sc_max, 1)
                        dve.wait_ge(exp_done, uu + 1)
                        own.after(dve, dve.reciprocal(ust[:, u, 6:8], ust[:, u, 4:6]))
                        for t in range(NT):
                            ins = dve.tensor_scalar(prob[:, u % 2, t * TOK:(t + 1) * TOK], prob[:, u % 2, t * TOK:(t + 1) * TOK],
                                                    ust[:, u, 6 + t:7 + t], None, ALU.mult)
                        ins.then_inc(p_ready, 1)
                    if u >= 8 or u % 2 == 1:
                        o_ = out_of(u)
                        dve.wait_ge(o_hi, N_OUT * r + o_ + 1)
                        dve.tensor_tensor(ot_lo[:, o_, :], ps[:, 6 + o_ % 2, 0:TOK], ot_hi[:, o_, :].bitcast(F32),
                                          ALU.subtract).then_inc(o_lo, 1)
                leave(dve, "dve"); n += 1

                enter(dve, "dve", n)
                stream(ph["gate"], r)
                leave(dve, "dve"); n += 1

                enter(dve, "dve", n)
                for ct in range(4):
                    for k in range(BR_SLABS):
                        gg = ph["branch"]["g0"] + BR_SLABS * ct + k
                        split_lo(gg, gg % RING)
                        turns(r, 0 if k % 3 == 2 else 1)
                    for side in range(2):
                        dve.wait_ge(slab_done, ph["branch"]["g0"] + BR_SLABS * ct + (BR_A, BR_SLABS)[side] + 2)
                        if ct and side == 0:
                            dve.wait_ge(merged_hi, 4 * r + ct)
                        dve.tensor_tensor((m1, m2)[side][:, :, :].rearrange("p a t -> p (a t)"),
                                          ps[:, 2 * side:2 * side + 2, :].rearrange("p b c -> p (b c)"),
                                          sg[:, KC * side + 4 * ct:KC * side + 4 * ct + 4, :].rearrange("p a t -> p (a t)"),
                                          ALU.mult).then_inc(acc_free, 1)
                    dve.wait_ge(acc_free, 2 + ph["branch"]["a0"] + 2 * ct + 2)
                    dve.tensor_tensor(m1[:, :, :], m1[:, :, :], m2[:, :, :], ALU.add).then_inc(merged, 1)
                    dve.wait_ge(merged_hi, 4 * r + ct + 1)
                    dve.tensor_tensor(ht_lo[:, 4 * ct:4 * ct + 4, :], m1[:, :, :], ht_hi[:, 4 * ct:4 * ct + 4, :].bitcast(F32), ALU.subtract)
                leave(dve, "dve"); n += 1

                enter(dve, "dve", n)
                dve.wait_ge(xres_in, 16 * (r + 1))
                dve.wait_ge(g2_in, 16 * (r + 1))

                def residual(ct):
                    dve.wait_ge(slab_done, ph["out"]["g0"] + SPC * (ct + 1) + 2)
                    dve.tensor_tensor(x1[:, :, ct * CT:(ct + 1) * CT], ps[:, 2 * (ct % 2):2 * (ct % 2) + 2, :],
                                      xin[:, :, ct * CT:(ct + 1) * CT], ALU.add).then_inc(acc_free, 1)
                for i in range(4 * SPC):
                    split_lo(ph["out"]["g0"] + i, i % RING)
                    turns(r, i % 2)
                    if i % SPC == 3 and i > SPC:
                        residual(i // SPC - 1)
                residual(3)
                dve.wait_ge(acc_free, 2 + ph["out"]["a0"] + 4)
                normalise(2 * r + 1, x1, h2[r])
                leave(dve, "dve"); n += 1

                enter(dve, "dve", n)
                stream(ph["pq"], r)
                leave(dve, "dve"); n += 1

                enter(dve, "dve", n)
                if r == 0:
                    own.after(dve, dve.memset(eidx[:, 2 * NT * SEL:], 0))
                for t in range(NT):
                    dve.wait_ge(s_out, 8 * r + 4 * t + 4)

                    def top16(values, val, idx, m):
                        for k in range(m):
                            ins = dve.max(val(k)[:, 0:8], values(k))
                        own.after(dve, ins)
                        turns(r, 3)
                        for k in range(m):
                            dve.max_index(idx(k)[:, 0:8], val(k)[:, 0:8], values(k))
                        turns(r, 3)
                        for k in range(m):
                            ins = dve.match_replace(values(k), val(k)[:, 0:8], values(k), LOWEST)
                        own.after(dve, ins)
                        for k in range(m):
                            ins = dve.max(val(k)[:, 8:16], values(k))
                        own.after(dve, ins)
                        for k in range(m):
                            ins = dve.max_index(idx(k)[:, 8:16], val(k)[:, 8:16], values(k))
                        own.after(dve, ins)
                        turns(r, 3)

                    top16(lambda k: s[:, t, k, :], lambda k: topv[:, k, :], lambda k: topi[:, k, :], 2 * PH)
                    own.after(dve, dve.tensor_copy(topf[:, :, :], topi[:, :, :]))
                    pairs_v = topv[:, :, :].rearrange("p (h c) k -> p h c k", c=2)
                    own.after(dve, dve.tensor_tensor(
                        cand[:, :, :].rearrange("p h (a b) -> p h a b", a=TOPK),
                        pairs_v[:, :, 0, :].unsqueeze(3).to_broadcast([P, PH, TOPK, TOPK]),
                        pairs_v[:, :, 1, :].unsqueeze(2).to_broadcast([P, PH, TOPK, TOPK]), ALU.add))
                    top16(lambda k: cand[:, k, :], lambda k: cv[:, k, :], lambda k: ci[:, k, :], PH)
                    dve.tensor_tensor(gsel[r][:, t, :].rearrange("p (h k) -> p h k", h=PH), cv[:, :, :],
                                      cv[:, :, 0:1].to_broadcast([P, PH, TOPK]), ALU.subtract).then_inc(shifted, 1)
                    cflat = ci[:, :, :].rearrange("p h k -> p (h k)")
                    pairs_i = topf[:, :, :].rearrange("p (h c) k -> p h c k", c=2)
                    for c in range(2):
                        turns(r, 3)
                        if c == 0:
                            own.after(dve, dve.tensor_scalar(cpart[:, :], cflat, 4, None, ALU.logical_shift_right))
                        else:
                            own.after(dve, dve.tensor_scalar(cpart[:, :], cflat, 15, None, ALU.bitwise_and))
                        own.after(dve, dve.tensor_copy(cpf[:, :], cpart[:, :]))
                        own.after(dve, dve.tensor_tensor(eq[:, :, :], cpf[:, :].unsqueeze(2).to_broadcast([P, SEL, TOPK]),
                                                         iota[:, 0:TOPK].unsqueeze(1).to_broadcast([P, SEL, TOPK]), ALU.is_equal))
                        eqh = eq[:, :, :].rearrange("p (h k) a -> p h k a", h=PH)
                        own.after(dve, dve.tensor_tensor(eqh, eqh, pairs_i[:, :, c, :].unsqueeze(2).to_broadcast([P, PH, TOPK, TOPK]),
                                                         ALU.mult))
                        own.after(dve, dve.tensor_reduce(keys[:, c, t, :], eq[:, :, :], AX.X, ALU.add))
                    if r == 0:
                        own.after(dve, dve.scalar_tensor_tensor(esum[:, :], keys[:, 0, t, :], float(NKEYS), keys[:, 1, t, :], ALU.mult, ALU.add))
                        for table in range(2):
                            k = (NT * table + t) * SEL
                            own.after(dve, dve.tensor_copy(eidx[:, k:k + SEL], esum[:, :]))
                    dve.wait_ge(exped, NT * r + t + 1)
                    gv = gsel[r][:, t, :].rearrange("p (h k) -> p h k", h=PH)
                    own.after(dve, dve.tensor_reduce(gsum[:, :], gv, AX.X, ALU.add))
                    own.after(dve, dve.reciprocal(gsum[:, :], gsum[:, :]))
                    own.after(dve, dve.tensor_tensor(gv, gv, gsum[:, :].unsqueeze(2).to_broadcast([P, PH, TOPK]), ALU.mult))
                if r == 1:
                    dve.drain().then_inc(sel_ready, 1)
                else:
                    dve.tensor_copy(stage_i[:, :], eidx[:, 0:8]).then_inc(staged, 1)
                leave(dve, "dve"); n += 1

            assert taken[0] == NT * SEL
            dve.wait_ge(copied, GROUPS + 1)
            dve.drain().then_inc(dots_done, 1)
            for h in range(HALVES):
                enter(dve, "dve", n)
                if h == 0:
                    dve.wait_ge(gelu_done, 1)
                    own.after(dve, dve.tensor_tensor(coef[:, :, :], coef[:, :, :], gsel[0][:, :, :], ALU.mult))
                with dve.Fori(0, TOK // 16) as i:
                    for c in range(2):
                        dve.wait_ge(picks_free, i * 2 + (TOK // 8 * h + c + 1))
                        for m in range(8):
                            tk = i * 16 + (8 * c + m)
                            dve.tensor_scalar(pick1[:, c, m, :], iota[:, HB * h:HB * h + HB], sel_t[:, 0, bass.ds(tk, 1)],
                                              sel_t[:, 2, bass.ds(tk, 1)], ALU.is_equal, ALU.mult)
                            ins = dve.tensor_scalar(pick2[:, c, m, :], iota[:, :], sel_t[:, 1, bass.ds(tk, 1)], None, ALU.is_equal)
                        ins.then_inc(picks_ready, 1)
                leave(dve, "dve"); n += 1

                enter(dve, "dve", n)
                if h == 0:
                    dve.wait_ge(x1_back, 16)
                g0 = table_g0[h][0]

                def weigh(b, par):
                    dve.wait_ge(a_free, b + (HB * h + 3))
                    cb = coefs[:, bass.ds(b, 1), :].rearrange("p a t -> p (a t)")
                    dve.tensor_tensor(cb, cb, ge[:, par, :], ALU.mult).then_inc(c_made, 1)

                def blocks(i, first=False):
                    for j in range(2 * BODY):
                        dve.wait_ge(hi_ready, i * (2 * BODY) + (g0 + j + 1))
                        dve.tensor_tensor(w_lo[:, j % 2, :, :], ps[:, 2 * (j % 2):2 * (j % 2) + 2, :],
                                          w_hi[:, j % 2, :, :].bitcast(F32), ALU.subtract).then_inc(lo_ready, 1)
                        if j % 2:
                            if not (first and j == 1):
                                weigh(i * BODY + (j // 2 - 1), (j // 2 - 1) % 2)
                            turn(i + 2 * BODY * h, j // 2, 1, h)
                blocks(0, True)
                with dve.Fori(1, HB // BODY) as i:
                    blocks(i)
                weigh(HB - 1, 1)
                leave(dve, "dve"); n += 1

                enter(dve, "dve", n)
                g0 = table_g0[h][1]
                with dve.Fori(0, HB // BODY) as i:
                    for j in range(2 * BODY):
                        split_lo(i * (2 * BODY) + (g0 + j), j)
                        if j % 2 == 0:
                            dve.wait_ge(c_hi_ready, i * BODY + (HB * h + j // 2 + 1))
                            dve.tensor_tensor(c_lo[:, j // 2 % 2, :],
                                              coefs[:, bass.ds(i * BODY + j // 2, 1), :].rearrange("p a t -> p (a t)"),
                                              c_hi[:, j // 2 % 2, :].bitcast(F32), ALU.subtract).then_inc(c_lo_ready, 1)
                        else:
                            turn(i + (2 * BODY * h + BODY), j // 2, 1, h)
                leave(dve, "dve"); n += 1

                enter(dve, "dve", n)
                dve.wait_ge(x1_in1, 16 * (h + 1))
                for t in range(NT):
                    for c in range(4):
                        ins = dve.tensor_tensor(total[:, t, c * CT:(c + 1) * CT], ps[:, 4 * t + c, :], total[:, t, c * CT:(c + 1) * CT], ALU.add)
                ins.then_inc(total_done, 1)
                leave(dve, "dve"); n += 1
            dve.drain().then_inc(acc_done, 1)

        @block.tensor
        def _(pe):
            pe.wait_ge(consts_in, 96)
            pe.sem_inc(slab_done, 2)
            pe.sem_inc(acc_free, 2)
            for sem in (picks_free, spread, a_free, c_made):
                pe.sem_inc(sem, 2)

            def slab(g_, j, ks, form, lhs, b0, first, last):
                hi, lo = lhs
                for part, (wt, other) in enumerate(((w_hi, hi), (w_hi, lo), (w_lo, hi))):
                    if part == 0:
                        pe.wait_ge(hi_ready, g_ + 1)
                    if part == 2:
                        pe.wait_ge(lo_ready, g_ + 1)
                    for kk in range(SK):
                        k = ks + kk
                        start = first and part == 0 and kk == 0
                        stop = last and part == 2 and kk == SK - 1
                        if form == "rows":
                            for t in range(NT):
                                ins = pe.matmul(ps[:, b0 + t, :], other[:, k, t * P:(t + 1) * P], wt[:, j % 2, kk, :],
                                                start=start, stop=stop)
                        else:
                            for q in range(4):
                                ins = pe.matmul(ps[:, b0 + q // 2, (q % 2) * TOK:(q % 2 + 1) * TOK],
                                                wt[:, j % 2, kk, q * P:(q + 1) * P], other[:, k, :],
                                                start=start and q % 2 == 0, stop=stop, skip_group_check=True)
                ins.then_inc(slab_done, 1)
                return ins

            def stream(ph, form):
                def pair(i):
                    for c in range(2):
                        pe.wait_ge(acc_free, i * 2 + (ph["a0"] + c + 1))
                        for j in range(SPC):
                            slab(i * (2 * SPC) + (ph["g0"] + SPC * c + j), j, SK * j, form, (ht_hi, ht_lo), 2 * c,
                                 j == 0, j == SPC - 1)
                with pe.Fori(0, ph["pairs"]) as i:
                    pair(i)

            def normalise(k, src):
                for t in range(NT):
                    pe.wait_ge(normed, k * NT + t + 1)
                    for q in range(4):
                        if t:
                            pe.wait_ge(turn_lo, k * 8 + q + 1)
                        for c in range(4):
                            ins = pe.transpose(ps[:, 4 + q, c * P:(c + 1) * P], src[:, t, (4 * q + c) * P:(4 * q + c + 1) * P], ident[:, :])
                        ins.then_inc(turned, 1)

            n = 0
            for r in range(REQ):
                ph = phases[r]
                enter(pe, "pe", n)
                normalise(2 * r, x1)
                leave(pe, "pe"); n += 1

                enter(pe, "pe", n)
                stream(ph["qkv"], "rows")
                leave(pe, "pe"); n += 1

                enter(pe, "pe", n)
                pe.wait_ge(roped, r + 1)
                for u in range(N_QK):
                    nh = 4 if u < 8 else 2
                    if u >= 2:
                        pe.wait_ge(qk_out, 9 * r + u - 1)
                    b0 = 4 * (u % 2)
                    for h in range(nh):
                        for t in range(NT):
                            ins = pe.transpose(ps[:, b0 + h // 2, (h % 2) * TOK + t * P:(h % 2) * TOK + (t + 1) * P],
                                               raw[:, u, t, h * DH:(h + 1) * DH], ident[:, :])
                    ins.then_inc(qk_turned, 1)
                pe.wait_ge(qk_out, 9 * (r + 1))

                def scores(u):
                    uu = N_UNITS * r + u
                    b0 = 2 * (u % 2)
                    if u >= 2:
                        pe.wait_ge(exp_done, uu - 1)
                    if u < 8:
                        hh, t = u // 2, u % 2
                        for g_ in range(A_GROUPS):
                            qh = 4 * g_ + hh
                            ins = pe.matmul(ps[:, b0 + g_ // 2, (g_ % 2) * TOK:(g_ % 2 + 1) * TOK],
                                            qkt(qh)[:, t * P:(t + 1) * P], qkt(12 + qh), start=True, stop=True)
                    else:
                        qh = u - 8
                        for t in range(NT):
                            ins = pe.matmul(ps[:, b0, t * TOK:(t + 1) * TOK], qkt(24 + qh)[:, t * P:(t + 1) * P],
                                            qkt(32 + qh // 4), start=True, stop=True)
                    ins.then_inc(sc_ready, 1)

                scores(0)
                for u in range(N_UNITS):
                    uu = N_UNITS * r + u
                    if u + 1 < N_UNITS:
                        scores(u + 1)
                    pe.wait_ge(p_ready, uu + 1)
                    if uu:
                        pe.wait_ge(pt_ready, uu)
                    if u < 8:
                        for k in range(6):
                            ins = pe.transpose(ps[:, 4 + k // 4, (k % 4) * P:(k % 4 + 1) * P],
                                               prob[:, u % 2, k * P:(k + 1) * P], ident[:, :])
                    else:
                        for t in range(NT):
                            for k in range(2):
                                ins = pe.transpose(ps[:, 4, k * TOK + t * P:k * TOK + (t + 1) * P],
                                                   prob[:, u % 2, t * TOK + k * P:t * TOK + (k + 1) * P], ident[:, :])
                    ins.then_inc(p_turned, 1)
                    if u >= 8 or u % 2 == 1:
                        o_ = out_of(u)
                        pe.wait_ge(pt_ready, uu + 1)
                        if o_ >= 2:
                            pe.wait_ge(o_lo, N_OUT * r + o_ - 1)
                        if u < 8:
                            vals = [raw[:, N_QK + k // 2, k % 2, o_ * DH:(o_ + 1) * DH] for k in range(6)]
                        else:
                            kv = 256 + (u - 8) // 4 * DH
                            vals = [raw[:, N_QK - 1, k, kv:kv + DH] for k in range(2)]
                        for k, val in enumerate(vals):
                            ins = pe.matmul(ps[:, 6 + o_ % 2, 0:TOK], val, pt[:, o_ % 2, k, :], start=(k == 0), stop=(k == len(vals) - 1))
                        ins.then_inc(pv_ready, 1)
                leave(pe, "pe"); n += 1

                enter(pe, "pe", n)
                stream(ph["gate"], "columns")
                leave(pe, "pe"); n += 1

                enter(pe, "pe", n)
                gg = ph["branch"]["g0"]
                for ct in range(4):
                    for side, (k0, ns) in enumerate(((0, BR_A), (4, BR_SLABS - BR_A))):
                        pe.wait_ge(acc_free, ph["branch"]["a0"] + 2 * ct + side + 1)
                        for j in range(ns):
                            slab(gg, gg, k0 + SK * j, "columns", (ot_hi, ot_lo), 2 * side, j == 0, j == ns - 1)
                            gg += 1
                leave(pe, "pe"); n += 1

                enter(pe, "pe", n)
                stream(ph["out"], "rows")
                normalise(2 * r + 1, h2[r])
                leave(pe, "pe"); n += 1

                enter(pe, "pe", n)
                stream(ph["pq"], "columns")
                pe.wait_ge(sk_in, 16 * (r + 1))
                for q in range(4):
                    for c in range(4):
                        ins = pe.transpose(ps[:, 4 + q, c * P:(c + 1) * P], skn[:, 4 * q + c, :], ident[:, :])
                    ins.then_inc(sk_turned, 1)
                leave(pe, "pe"); n += 1

                enter(pe, "pe", n)
                for q in range(8):
                    t, c = q // 4, q % 4
                    for k in range(4):
                        ins = pe.matmul(ps[:, q, k * P:(k + 1) * P], qt[:, 4 * c + k, t * P:(t + 1) * P], skt[:, 4 * c + k, :],
                                        start=True, stop=True)
                    ins.then_inc(s_ready, 1)
                if r == 1:
                    pe.wait_ge(sel_ready, 1)
                    for k in range(3):
                        for t in range(NT):
                            src = keys[:, k, t, :] if k < 2 else gsel[1][:, t, :]
                            c0 = k % 2 * TOK + t * P
                            ins = pe.transpose(ps[:, k // 2, c0:c0 + P], src, ident[:, :])
                    ins.then_inc(sel_turned, 1)
                leave(pe, "pe"); n += 1

            pe.wait_ge(zero_ready, 1)
            for h in range(HALVES):
                enter(pe, "pe", n)
                with pe.Fori(0, TOK // 16) as i:
                    for c in range(2):
                        pe.wait_ge(picks_ready, i * 2 + (TOK // 8 * h + c + 1))
                        pe.wait_ge(spread, i * 2 + (TOK // 8 * h + c + 1))
                        for m in range(8):
                            ins = pe.matmul(ps[:, c, m * HB:(m + 1) * HB], pick2[:, c, m, :], pick1[:, c, m, :], start=True, stop=True)
                        ins.then_inc(picks_free, 1)
                leave(pe, "pe"); n += 1

                enter(pe, "pe", n)
                g0 = table_g0[h][0]

                def turn_block(G, j):
                    pe.wait_ge(w_loaded[j % RING], (G + (g0 - j % RING)) * (16 // RING) + 16)
                    pe.wait_ge(lo_ready, G + (g0 - 1))
                    for k in range(8):
                        ins = pe.transpose(ps[:, 2 * (j % 2) + k // 4, k % 4 * P:(k % 4 + 1) * P],
                                           w[:, j % RING, k // 4, k % 4 * P:(k % 4 + 1) * P], ident[:, :])
                    ins.then_inc(u_turned, 1)

                def blocks(i, last=False):
                    for j in range(2 * BODY):
                        if not (last and j == 2 * BODY - 1):
                            turn_block(i * (2 * BODY) + (j + 1), j + 1)
                        c, b = j % 2, j // 2
                        if c == 0:
                            pe.wait_ge(a_free, i * BODY + (HB * h + b + 1))
                        for part, (wt, other) in enumerate(((w_hi, ht_hi), (w_hi, ht_lo), (w_lo, ht_hi))):
                            if part == 0:
                                pe.wait_ge(hi_ready, i * (2 * BODY) + (g0 + j + 1))
                            if part == 2:
                                pe.wait_ge(lo_ready, i * (2 * BODY) + (g0 + j + 1))
                            for k in range(8):
                                ins = pe.matmul(ps[:, 4 + b % 2, 0:TOK], wt[:, j % 2, k // 4, k % 4 * P:(k % 4 + 1) * P],
                                                other[:, 8 * c + k, :], start=(c == 0 and part == 0 and k == 0),
                                                stop=(c == 1 and part == 2 and k == 7))
                        ins.then_inc(slab_done, 1)
                turn_block(0, 0)
                with pe.Fori(0, HB // BODY - 1) as i:
                    blocks(i)
                blocks(HB // BODY - 1, True)
                leave(pe, "pe"); n += 1

                enter(pe, "pe", n)
                g0 = table_g0[h][1]
                for k in range(8):
                    pe.matmul(ps[:, k, :], zeros[:, 0:P], zeros[:, :], start=True, stop=True)
                with pe.Fori(0, HB // BODY) as i:
                    for j in range(2 * BODY):
                        c, b = j % 2, j // 2
                        for part, (cf, wt) in enumerate(((c_hi, w_hi), (c_lo, w_hi), (c_hi, w_lo))):
                            if part == 0:
                                pe.wait_ge(hi_ready, i * (2 * BODY) + (g0 + j + 1))
                                pe.wait_ge(c_hi_ready, i * BODY + (HB * h + b + 1))
                            if part == 1:
                                pe.wait_ge(c_lo_ready, i * BODY + (HB * h + b + 1))
                            if part == 2:
                                pe.wait_ge(lo_ready, i * (2 * BODY) + (g0 + j + 1))
                            for t in range(NT):
                                for k in range(2):
                                    ins = pe.matmul(ps[:, 4 * t + 2 * c + k, :], cf[:, b % 2, t * P:(t + 1) * P], wt[:, j % 2, k, :],
                                                    start=False, stop=True, skip_group_check=True)
                        ins.then_inc(slab_done, 1)
                leave(pe, "pe"); n += 1
                enter(pe, "pe", n); leave(pe, "pe"); n += 1


def kernel(**inputs):
    import concourse.bacc as bacc
    from concourse.bass_utils import run_bass_kernel_spmd as run

    f = lambda name: np.ascontiguousarray(inputs[name][0])
    rows = lambda v, n: np.ascontiguousarray(np.broadcast_to(v, (n,) + v.shape))
    q = np.arange(TOK)
    near = np.abs(q[:, None] - q[None, :])
    allowed = np.concatenate([near <= 64, near % 4 == 0, near % 16 == 0], axis=1)
    mask = np.where(allowed, 0.0, NEG).astype(np.float32).reshape(NT, P, A_GROUPS * TOK).transpose(1, 0, 2)

    def table(pos, dim, theta):
        inv = np.float32(theta) ** (-(np.arange(0, dim, 2, dtype=np.float32) / np.float32(dim)))
        ang = pos.astype(np.float32)[:, None] * inv[None, :].astype(np.float32)
        return np.stack([np.cos(ang), np.sin(ang)]).astype(np.float32)
    rope_a = table(q, 32, 500000.0).reshape(2, NT, P, ROT).transpose(2, 0, 1, 3)
    rope_b = np.stack([table(q // 64, 64, 10000.0), table(q % 64, 64, 10000.0)], axis=2).reshape(2, NT, P, 2, 32).transpose(2, 0, 1, 3, 4)
    gains = np.stack([f("qn_a"), f("kn_a"), f("qn_b"), f("kn_b")])
    arrays = {
        "x": np.concatenate([inputs["x_prompt"], inputs["x_sample"]], axis=0),
        "g_mix_b": rows(f("g_mix"), P), "g_ffn_b": rows(f("g_ffn"), P), "w_in": f("w_in"), "gains": rows(gains, P),
        "w_br_a": f("w_br_a"), "w_br_b": f("w_br_b"), "w_out": f("w_out"), "w_pq": f("w_pq"),
        "sub_keys": f("sub_keys").reshape(2 * PH, NKEYS, P), "u_emb": f("u_emb"), "v_emb": f("v_emb"),
        "ident_c": np.eye(P, dtype=np.float32), "mask_c": mask, "rope_a_c": rope_a, "rope_b_c": rope_b,
        "iota_c": rows(np.arange(NKEYS, dtype=np.float32), P),
    }
    arrays = {k: np.ascontiguousarray(v) for k, v in arrays.items()}
    nc = bacc.Bacc("TRN2", target_bir_lowering=False, num_devices=1)
    args = [nc.dram_tensor(k, v.shape, F32, kind="ExternalInput").ap() for k, v in arrays.items()]
    y = nc.dram_tensor("y", (REQ, TOK, D), F32, kind="ExternalOutput").ap()
    encoder(nc, *args, y)
    out = run(nc, [arrays], core_ids=[0]).results[0]["y"]
    return out[0:1], out[1:2]
```

```python
import numpy as np
import concourse.bass as bass
from concourse import mybir

F32 = mybir.dt.float32
F32R = mybir.dt.float32r
BF16 = mybir.dt.bfloat16
U32 = mybir.dt.uint32
ALU = mybir.AluOpType
ACT = mybir.ActivationFunctionType
AX = mybir.AxisListType

P = 128
D = 2048
KC = D // P
TOK = 256
NT = TOK // P
REQ = 2
BR_A, BR_SLABS = 2, 6
DH = 128
SCALE = DH ** -0.5
EPS = 1e-6
CT = 512
SK = 2
SPC = KC // SK
RING = 4
ROWS = 4
A_HEADS, A_MERGED, A_GROUPS = 12, 4, 3
B_HEADS, B_KV = 8, 2
QKV_CT = 12
GATE_CT = 8
ROT = 16
PH, NKEYS, TOPK = 8, 128, 16
SEL = PH * TOPK
GROUPS = NT * SEL // 8
HALVES, HB = 2, NKEYS // 2
BODY = 8
SPAN = 8
EARLY = HB // 2
G_TURNS, U_TURNS, V_TURNS = TOK // SPAN, (48, 80), 48
NEG = -1.0e30
LOWEST = -3.0e38


TILE_ORDER = (0, 3, 1, 4, 2, 5, 9, 10, 11, 6, 7, 8)
N_QK = 9
QK_PAIRS = 5
QK_OPS = 14
SQUARES = 4 * (QK_PAIRS - 1) + NT
N_UNITS = 16
N_OUT = 12


def out_of(u):
    return u // 2 if u < 8 else u - 4


class Counter:

    def __init__(self, sem):
        self.sem, self.n, self.base = sem, 0, 0

    def after(self, eng, ins):
        self.n += 1
        ins.then_inc(self.sem, 1)
        eng.wait_ge(self.sem, self.base + self.n)


def encoder(nc, x, g_mix_b, g_ffn_b, w_in, gains, w_br_a, w_br_b, w_out, w_pq, sub_keys, u_emb, v_emb,
            ident_c, mask_c, rope_a_c, rope_b_c, iota_c, y):
    base = 16512
    place = {}

    def at(name, offset, shape, dtype):
        place[name] = nc.alloc_sbuf_tensor_at(name, [P] + shape, dtype, offset=offset)
        return place[name]

    o = base
    ident = at("ident", o, [P], F32); o += 512
    rope_a = at("rope_a", o, [2, NT, ROT], F32); o += 256
    rope_b = at("rope_b", o, [2, NT, 2, 32], F32); o += 1024
    gain = at("gain", o, [4, DH], F32); o += 2048
    mask = at("mask", o, [NT, A_GROUPS * TOK], F32)
    sel_t = at("sel_t", o, [3, TOK], F32)
    weight_split = at("weight_split", o + 3072, [2, TOK], F32R); o += 6144
    iota = at("iota", o, [NKEYS], F32); o += 512
    tick = at("tick", o, [4], F32); o += 32
    stat = at("stat", o, [16], F32); o += 64
    eidx = at("eidx", o, [2 * NT * SEL + 8], U32); o += 2080
    gsel = [at(f"gsel{r}", o + 1024 * r, [NT, SEL], F32) for r in range(REQ)]; o += 2048
    zeros = at("zeros", o, [CT], BF16); o += 1024
    dots = at("dots", o, [NT, SEL], F32); o += 1024
    coef = at("coef", o, [NT, SEL], F32); o += 1024
    stage_i = at("stage_i", o, [8], U32); o += 32
    stage_d = at("stage_d", o, [8], F32); o += 32
    R_HT = o; o += 32768
    R_RAW = o; o += 49152
    R_OT = o; o += 24576
    R_W = o; o += 16384
    R_SPLIT = o; o += 19968
    R_H2 = o; o += 16384
    R_ROWS = o; o += 32768

    ht_hi = at("ht_hi", R_HT, [KC, TOK], F32R)
    ht_lo = at("ht_lo", R_HT + 16384, [KC, TOK], F32R)
    raw = at("raw", R_RAW, [QKV_CT, NT, CT], F32)

    def qkt(tile, head):
        if tile < N_QK - 1:
            return raw[:, tile, :, :].rearrange("p t c -> p (t c)")[:, head * TOK:(head + 1) * TOK]
        return raw[:, tile, head, 0:TOK]

    ot_hi = at("ot_hi", R_OT, [12, TOK], F32R)
    ot_lo = at("ot_lo", R_OT + 12288, [12, TOK], F32R)
    xin = at("xin", R_RAW, [NT, D], F32)
    x1 = at("x1", R_RAW + 16384, [NT, D], F32)
    gvec = at("gvec", R_RAW + 32768, [D], F32)
    junk = at("junk", R_RAW + 40960, [D], F32)
    sg = at("sg", R_RAW, [2 * KC, TOK], F32)
    m1 = at("m1", R_RAW + 32768, [4, TOK], F32)
    m2 = at("m2", R_RAW + 36864, [4, TOK], F32)
    skn = at("skn", R_RAW, [2 * PH, P], F32)
    skt = at("skt", R_RAW + 8192, [2 * PH, P], F32)
    qt = at("qt", R_RAW + 16384, [2 * PH, TOK], F32)
    w = at("w", R_W, [RING, SK, CT], F32)
    w_hi = at("w_hi", R_SPLIT, [2, SK, CT], F32R)
    w_lo = at("w_lo", R_SPLIT + 8192, [2, SK, CT], F32R)
    h2 = [at("h2_0", R_H2, [NT, D], F32), at("h2_1", R_OT, [NT, D], F32)]
    prob = at("prob", R_SPLIT, [2, A_GROUPS * TOK], F32)
    pt = at("pt", R_SPLIT + 6144, [2, 6, TOK], F32)
    rt = at("rt", R_OT, [4, 256], F32)
    sq = at("sq", R_OT + 4096, [4 * 4, DH], F32)
    ss = at("ss", R_OT + 12288, [16], F32)
    root = at("root", R_OT + 12352, [16], F32)
    rs = at("rs", R_OT + 12416, [16], F32)
    rtmp = at("rtmp", R_OT + 12480, [16], F32)
    ust = at("ust", R_SPLIT + 19296, [N_UNITS, 8], F32)
    s = at("s", R_OT, [NT, 2 * PH, NKEYS], F32)
    cand = at("cand", R_RAW + 40960, [PH, TOPK * TOPK], F32)
    eq = at("eq", R_OT + 16384, [PH * TOPK, TOPK], F32)
    topv = at("topv", R_RAW + 32768, [2 * PH, TOPK], F32)
    topi = at("topi", R_RAW + 33792, [2 * PH, TOPK], U32)
    topf = at("topf", R_RAW + 34816, [2 * PH, TOPK], F32)
    cv = at("cv", R_RAW + 35840, [PH, TOPK], F32)
    ci = at("ci", R_RAW + 36352, [PH, TOPK], U32)
    cpart = at("cpart", R_RAW + 36864, [SEL], U32)
    cpf = at("cpf", R_RAW + 37376, [SEL], F32)
    keys = at("keys", R_RAW + 37888, [2, NT, SEL], F32)
    esum = at("esum", R_RAW + 39936, [SEL], F32)
    gsum = at("gsum", R_RAW + 40448, [PH], F32)
    rows = at("rows", R_ROWS, [ROWS, D], F32)
    acc = at("acc", R_H2, [NT, D], F32)
    coefs = at("coefs", R_RAW, [HB, TOK], F32)
    c_hi = at("c_hi", R_RAW + 65536, [2, TOK], F32R)
    c_lo = at("c_lo", R_RAW + 67584, [2, TOK], F32R)
    ge = at("ge", R_RAW + 69632, [2, TOK], F32)
    total = at("total", R_RAW, [NT, D], F32)
    pick1 = at("pick1", R_SPLIT, [2, 2, SPAN, HB], F32R)
    pick2 = at("pick2", R_SPLIT + 8192, [2, SPAN, NKEYS], F32R)
    match1 = at("match1", R_SPLIT + 16384, [2, SPAN, HB], BF16)

    ps = nc.alloc_psum_tensor("ps", [P, 8, 512], F32)
    S = nc.alloc_semaphore
    consts_in = S("consts_in")
    x_in, g_in, xres_in, g2_in, sk_in, y_out, x1_back = (S(n) for n in ("x_in", "g_in", "xres_in", "g2_in", "sk_in", "y_out", "x1_back"))
    w_loaded = [S(f"w_loaded{j}") for j in range(RING)]
    hi_ready, lo_ready, slab_done = S("hi_ready"), S("lo_ready"), S("slab_done")
    acc_free = S("acc_free")
    done = {n: S(f"done_{n}") for n in ("pe", "act", "dve")}
    dve_own, dve_qk_own = S("dve_own"), S("dve_qk_own")
    used, copied, staged = S("used"), S("copied"), S("staged")
    ticked, acc_done, x1_in1 = S("ticked"), S("acc_done"), S("x1_in1")
    zero_ready, sel_ready, sel_turned = S("zero_ready"), S("sel_ready"), S("sel_turned")
    picks_free, weighed = S("picks_free"), S("weighed")
    matched, picks_ready, spread = S("matched"), S("picks_ready"), S("spread")
    u_turned, a_free, c_made, c_hi_ready, c_lo_ready, total_done, y_half = (
        S(n) for n in ("u_turned", "a_free", "c_made", "c_hi_ready", "c_lo_ready", "total_done", "y_half"))
    sum_ready, mean_ready, root_ready = S("sum_ready"), S("mean_ready"), S("root_ready")
    normed, turned, turn_hi, turn_lo = S("normed"), S("turned"), S("turn_hi"), S("turn_lo")
    eps_ready, squared, rooted, roped, qk_turned, qk_out = (
        S(n) for n in ("eps_ready", "squared", "rooted", "roped", "qk_turned", "qk_out"))
    sc_ready, sc_max, exp_done, p_ready, p_turned, pt_ready, pv_ready, o_hi, o_lo = (
        S(n) for n in ("sc_ready", "sc_max", "exp_done", "p_ready", "p_turned", "pt_ready", "pv_ready", "o_hi", "o_lo"))
    merged, merged_hi = S("merged"), S("merged_hi")
    sk_turned, sk_out, s_ready, s_out, shifted, exped = (S(n) for n in ("sk_turned", "sk_out", "s_ready", "s_out", "shifted", "exped"))
    row_in = [S(f"row_in{j}") for j in range(ROWS)]
    dots_done, gelu_done = S("dots_done"), S("gelu_done")

    def slabs(columns, slab_base, acc_base):
        return dict(pairs=columns // 2, g0=slab_base, a0=acc_base)

    phases, g, a = [], 0, 0
    for r in range(REQ):
        ph = {}
        for name, n in (("qkv", QKV_CT), ("gate", GATE_CT)):
            ph[name] = slabs(n, g, a); g += SPC * n; a += n
        ph["branch"] = dict(g0=g, a0=a); g += 4 * BR_SLABS; a += 8
        for name, n in (("out", 4), ("pq", 4)):
            ph[name] = slabs(n, g, a); g += SPC * n; a += n
        phases.append(ph)
    table_g0 = [[g + 4 * HB * h, g + 4 * HB * h + 2 * HB] for h in range(HALVES)]

    w_view = {
        "qkv": (w_in.rearrange("(s k p) n -> s p k n", k=SK, p=P), 0),
        "gate": (w_in.rearrange("(s k p) n -> s p k n", k=SK, p=P), QKV_CT * CT),
        "out": (w_out.rearrange("(s k p) n -> s p k n", k=SK, p=P), 0),
        "pq": (w_pq.rearrange("(s k p) n -> s p k n", k=SK, p=P), 0),
    }
    bra = w_br_a.rearrange("(s k p) n -> s p k n", k=SK, p=P)
    brb = w_br_b.rearrange("(s k p) n -> s p k n", k=SK, p=P)

    def enter(eng, me, n):
        for other in done:
            if other != me and n:
                eng.wait_ge(done[other], n)

    def leave(eng, me):
        eng.drain().then_inc(done[me], 1)

    block_cm = nc.Block()
    with block_cm as block:

        @block.sync
        def _(sp):
            def load(src, slot, g_):
                if not isinstance(g_, int) or g_ >= RING:
                    sp.wait_ge(lo_ready, g_ - RING + 1)
                sp.dma_start(w[:, slot, :, :], src).then_inc(w_loaded[slot], 16)

            def stream(name, ph):
                view, col0 = w_view[name]

                def pair(i, tiles=None):
                    for c in range(2):
                        for j in range(SPC):
                            g_ = i * (2 * SPC) + (ph["g0"] + SPC * c + j)
                            n0 = i * (2 * CT) + (col0 + c * CT) if tiles is None else tiles(i, c)
                            load(view[j, :, :, bass.ds(n0, CT)], j % RING, g_)
                if name == "qkv":
                    group = lambda i, c: i * CT + c * A_GROUPS * CT
                    pair(0, group)
                    with sp.Fori(1, A_GROUPS) as i:
                        pair(i, group)
                    for i in range(A_GROUPS, QKV_CT // 2):
                        pair(i, lambda i, c: TILE_ORDER[2 * i + c] * CT)
                else:
                    pair(0)
                    with sp.Fori(1, ph["pairs"]) as i:
                        pair(i)

            for r in range(REQ):
                ph = phases[r]
                stream("qkv", ph["qkv"])
                stream("gate", ph["gate"])
                n = ph["branch"]["g0"]
                for ct in range(4):
                    for src in [bra[k] for k in range(BR_A)] + [brb[k] for k in range(BR_SLABS - BR_A)]:
                        load(src[:, :, ct * CT:(ct + 1) * CT], n % RING, n)
                        n += 1
                stream("out", ph["out"])
                stream("pq", ph["pq"])
            for h in range(HALVES):
                for table, emb in enumerate((u_emb, v_emb)):
                    blocks = emb.rearrange("(b p) d -> p b d", p=P)
                    with sp.Fori(0, HB // BODY) as i:
                        for j in range(2 * BODY):
                            sp.wait_ge(lo_ready, i * (2 * BODY) + (table_g0[h][table] + j - RING + 1))
                            sp.dma_start(w[:, j % RING, :, :].rearrange("p k c -> p (k c)").unsqueeze(1),
                                         blocks[:, bass.ds(i * BODY + (HB * h + j // 2), 1), D // 2 * (j % 2):D // 2 * (j % 2 + 1)]
                                         ).then_inc(w_loaded[j % RING], 16)

        @block.gpsimd
        def _(pool):
            pool.wait_ge(consts_in, 96)
            pool.wait_ge(staged, 1)

            def gather(K, j, table):
                pool.wait_ge(used, K * 8 + (8 * GROUPS * table + j + 2))
                pool.tensor_tensor(tick[:, j // 2:j // 2 + 1], iota[:, 0:1], iota[:, 0:1], ALU.add).then_inc(ticked, 1)
                for jj in (j, j + 1):
                    pool.indirect_dma_start(rows[:, jj % ROWS, :], None, (u_emb, v_emb)[table],
                                            bass.IndirectOffsetOnAxis(ap=stage_i[:, jj:jj + 1], axis=0)).then_inc(row_in[jj % ROWS], 16)

            for table in range(2):
                with pool.Fori(0, GROUPS) as i:
                    for j in range(0, 8, 2):
                        gather(i, j, table)

        @block.scalar
        def _(act):
            xs = [x[r].rearrange("(t p) d -> p t d", p=P) for r in range(REQ)]
            act.dma_start(xin[:, :, :], xs[0]).then_inc(x_in, 16)
            for dst, src in ((ident[:, :], ident_c), (rope_a[:, :, :, :], rope_a_c), (rope_b[:, :, :, :, :], rope_b_c),
                             (gain[:, :, :], gains), (mask[:, :, :], mask_c), (iota[:, :], iota_c)):
                act.dma_start(dst, src).then_inc(consts_in, 16)
                if src is ident_c:
                    act.dma_start(gvec[:, :], g_mix_b).then_inc(g_in, 16)

            def split_hi(g_, j):
                act.wait_ge(w_loaded[j % RING], loads(g_, j))
                act.wait_ge(slab_done, g_ + 1)
                act.activation(w_hi[:, j % 2, :, :], w[:, j % RING, :, :], ACT.Copy).then_inc(hi_ready, 1)

            def loads(g_, j):
                return (g_ - (j % RING)) * (16 // RING) + 16

            def stream(ph, evacuate, beside=lambda i, j: None):
                def pair(i, first=False):
                    for c in range(2):
                        for j in range(SPC):
                            split_hi(i * (2 * SPC) + (ph["g0"] + SPC * c + j), j)
                            if j == 3 and not (first and c == 0):
                                out(i * 2 + (c - 1), 1 - c)
                            if c == 0:
                                beside(i, j)

                def out(ct, side):
                    act.wait_ge(slab_done, ct * SPC + (ph["g0"] + SPC + 2))
                    evacuate(ct, side).then_inc(acc_free, 1)
                pair(0, True)
                if ph is phases[0]["qkv"] or ph is phases[1]["qkv"]:
                    with act.Fori(1, A_GROUPS + 1) as i:
                        pair(i)
                    for i in range(A_GROUPS + 1, QKV_CT // 2):
                        pair(i)
                else:
                    with act.Fori(1, ph["pairs"]) as i:
                        pair(i)
                out(2 * ph["pairs"] - 1, 1)

            act.wait_ge(eps_ready, 1)

            def normalise(k):
                for t in range(NT):
                    if t:
                        act.wait_ge(sum_ready, NT * k + t)
                    act.activation(junk[:, :], (xin if k % 2 == 0 else x1)[:, t, :], ACT.Square,
                                   accum_out=stat[:, t:t + 1]).then_inc(sum_ready, 1)
                act.wait_ge(mean_ready, k + 1)
                act.activation(stat[:, 4:6], stat[:, 2:4], ACT.Sqrt).then_inc(root_ready, 1)
                for t in range(NT):
                    for q in range(4):
                        m = k * 8 + t * 4 + q
                        act.wait_ge(turned, m + 1)
                        act.activation(ht_hi[:, 4 * q:4 * q + 4, t * P:(t + 1) * P],
                                       ps[:, 4 + q, :].rearrange("p (k t) -> p k t", k=4), ACT.Copy).then_inc(turn_hi, 1)

            def u_blocks(h, b0, count, late):
                g0 = table_g0[h][0] + 2 * b0

                def activate(b, par):
                    act.wait_ge(slab_done, b * 2 + (g0 + 2 + 2))
                    if late:
                        act.wait_ge(c_made, b + (HB * h + b0 - EARLY + 1))
                        out = ge[:, par, :]
                    else:
                        out = coefs[:, bass.ds(b + b0, 1), :].rearrange("p a t -> p (a t)")
                    act.activation(out, ps[:, 4 + par, 0:TOK], ACT.Gelu).then_inc(a_free, 1)

                def blocks(i, first=False):
                    for j in range(2 * BODY):
                        act.wait_ge(u_turned, i * (2 * BODY) + (2 * (HB * h + b0) + j + 1))
                        act.wait_ge(slab_done, i * (2 * BODY) + (g0 + j + 1))
                        act.activation(w_hi[:, j % 2, :, :], ps[:, 2 * (j % 2):2 * (j % 2) + 2, :], ACT.Copy).then_inc(hi_ready, 1)
                        if j % 2 == 0 and not (first and j == 0):
                            activate(i * BODY + (j // 2 - 1), (j // 2 - 1) % 2)
                blocks(0, True)
                with act.Fori(1, count // BODY) as i:
                    blocks(i)
                activate(count - 1, 1)

            n = 0
            for r in range(REQ):
                ph = phases[r]
                xr = xs[r]
                yr = y[r].rearrange("(t p) d -> p t d", p=P)
                enter(act, "act", n)
                if r:
                    act.dma_start(gvec[:, :], g_mix_b).then_inc(g_in, 16)
                act.wait_ge(x_in, 16 * (r + 1))
                normalise(2 * r)
                leave(act, "act"); n += 1

                enter(act, "act", n)

                def squares(i, j):
                    tiles = 2
                    if isinstance(i, int):
                        tiles = (0, 2, 2, 2, 2, 1)[i]
                    if j < 4 or not tiles:
                        return
                    heads = 4 if tiles == 2 else B_KV
                    if j == 4:
                        act.wait_ge(roped, i + QK_PAIRS * r)
                    c, t = (j - 4) // 2, j % 2
                    if c < tiles:
                        for h in range(heads):
                            k = 4 * (j - 4) + h if tiles == 2 else t * heads + h
                            ins = act.activation(sq[:, 4 * (j - 4) + h, :], raw[:, bass.ds(i * 2 + (c - 2), 1), t, h * DH:(h + 1) * DH].rearrange("p a d -> p (a d)"),
                                                 ACT.Square, accum_out=ss[:, k:k + 1])
                        ins.then_inc(squared, 1)
                    if j == 7:
                        n_ = 16 if tiles == 2 else NT * heads
                        act.wait_ge(squared, i * 4 + (SQUARES * r) if tiles == 2 else SQUARES * (r + 1))
                        act.activation(root[:, 0:n_], ss[:, 0:n_], ACT.Sqrt, scale=1.0 / DH, bias=stat[:, 12:13]).then_inc(rooted, 1)
                stream(ph["qkv"], lambda ct, side: act.activation(
                    raw[:, bass.ds(ct, 1), :, :].rearrange("p a t c -> p (a t c)"),
                    ps[:, 2 * side:2 * side + 2, :].rearrange("p b c -> p (b c)"), ACT.Copy), squares)
                leave(act, "act"); n += 1

                enter(act, "act", n)
                for u in range(N_QK):
                    act.wait_ge(qk_turned, 9 * r + u + 1)
                    b0 = 4 * (u % 2)
                    if u < 8:
                        act.activation(raw[:, u, :, :], ps[:, b0:b0 + 2, :], ACT.Copy).then_inc(qk_out, 1)
                    else:
                        act.activation(raw[:, u, :, 0:TOK], ps[:, b0, :].rearrange("p (h t) -> p h t", h=2),
                                       ACT.Copy).then_inc(qk_out, 1)

                def exponentials(u):
                    act.wait_ge(sc_max, N_UNITS * r + u + 1)
                    if u < 8:
                        act.activation(prob[:, u % 2, :], prob[:, u % 2, :], ACT.Exp, bias=ust[:, u, 2:3], scale=SCALE,
                                       accum_out=ust[:, u, 4:5]).then_inc(exp_done, 1)
                    else:
                        b0 = 2 * (u % 2)
                        for t in range(NT):
                            ins = act.activation(prob[:, u % 2, t * TOK:(t + 1) * TOK], ps[:, b0, t * TOK:(t + 1) * TOK],
                                                 ACT.Exp, bias=ust[:, u, 2 + t:3 + t], scale=SCALE,
                                                 accum_out=ust[:, u, 4 + t:5 + t])
                        ins.then_inc(exp_done, 1)

                def result(u):
                    if u >= 8 or u % 2 == 1:
                        o_ = out_of(u)
                        act.wait_ge(pv_ready, N_OUT * r + o_ + 1)
                        act.activation(ot_hi[:, o_, :], ps[:, 6 + o_ % 2, 0:TOK], ACT.Copy).then_inc(o_hi, 1)

                exponentials(0)
                for u in range(N_UNITS):
                    if u + 1 < N_UNITS:
                        exponentials(u + 1)
                    act.wait_ge(p_turned, N_UNITS * r + u + 1)
                    o_, oi = out_of(u), N_OUT * r + out_of(u)
                    t = u % 2
                    if o_ >= 2 and (u >= 8 or t == 0):
                        act.wait_ge(pv_ready, oi - 1)
                    if u < 8:
                        act.activation(pt[:, o_ % 2, :, t * P:(t + 1) * P],
                                       ps[:, 4:6, :].rearrange("p b c -> p (b c)")[:, 0:768].rearrange("p (k q) -> p k q", k=6),
                                       ACT.Copy).then_inc(pt_ready, 1)
                    else:
                        act.activation(pt[:, o_ % 2, 0:2, :], ps[:, 4, :].rearrange("p (k q) -> p k q", k=2),
                                       ACT.Copy).then_inc(pt_ready, 1)
                    if u:
                        result(u - 1)
                result(N_UNITS - 1)
                leave(act, "act"); n += 1

                enter(act, "act", n)
                stream(ph["gate"], lambda ct, side: act.activation(
                    sg[:, bass.ds(ct * 4, 4), :].rearrange("p a t -> p (a t)"),
                    ps[:, 2 * side:2 * side + 2, :].rearrange("p b c -> p (b c)"), ACT.Sigmoid))
                leave(act, "act"); n += 1

                enter(act, "act", n)
                for ct in range(4):
                    for k in range(BR_SLABS):
                        gg = ph["branch"]["g0"] + BR_SLABS * ct + k
                        split_hi(gg, gg % RING)
                    act.wait_ge(merged, 4 * r + ct + 1)
                    act.activation(ht_hi[:, 4 * ct:4 * ct + 4, :], m1[:, :, :], ACT.Copy).then_inc(merged_hi, 1)
                leave(act, "act"); n += 1

                enter(act, "act", n)
                act.dma_start(xin[:, :, :], xr).then_inc(xres_in, 16)
                act.dma_start(gvec[:, :], g_ffn_b).then_inc(g2_in, 16)
                for i in range(2 * ph["out"]["pairs"] * SPC):
                    split_hi(ph["out"]["g0"] + i, i % RING)
                act.wait_ge(acc_free, 2 + ph["out"]["a0"] + 4)
                normalise(2 * r + 1)
                leave(act, "act"); n += 1

                enter(act, "act", n)
                act.dma_start(yr, x1[:, :, :]).then_inc(y_out, 16)
                act.dma_start(skn[:, :, :], sub_keys.rearrange("c n d -> n c d")).then_inc(sk_in, 16)
                for i in range(2 * ph["pq"]["pairs"] * SPC):
                    split_hi(ph["pq"]["g0"] + i, i % RING)
                    if i % SPC == 3 and i > SPC:
                        ct = i // SPC - 1
                        if ct == 0:
                            act.wait_ge(y_out, 16 * (r + 1))
                        act.wait_ge(slab_done, ph["pq"]["g0"] + SPC * (ct + 1) + 2)
                        act.activation(qt[:, 4 * ct:4 * ct + 4, :].rearrange("p a t -> p (a t)"),
                                       ps[:, 2 * (ct % 2):2 * (ct % 2) + 2, :].rearrange("p b c -> p (b c)"),
                                       ACT.Copy).then_inc(acc_free, 1)
                act.wait_ge(slab_done, ph["pq"]["g0"] + SPC * 4 + 2)
                act.activation(qt[:, 12:16, :].rearrange("p a t -> p (a t)"),
                               ps[:, 2:4, :].rearrange("p b c -> p (b c)"), ACT.Copy).then_inc(acc_free, 1)
                for q in range(4):
                    act.wait_ge(sk_turned, 4 * r + q + 1)
                    act.activation(skt[:, 4 * q:4 * q + 4, :].rearrange("p a n -> p (a n)"), ps[:, 4 + q, :],
                                   ACT.Copy).then_inc(sk_out, 1)
                leave(act, "act"); n += 1

                enter(act, "act", n)
                for q in range(8):
                    act.wait_ge(s_ready, 8 * r + q + 1)
                    t, c = q // 4, q % 4
                    act.activation(s[:, t, 4 * c:4 * c + 4, :].rearrange("p a n -> p (a n)"), ps[:, q, :],
                                   ACT.Copy).then_inc(s_out, 1)
                if r == 0:
                    act.wait_ge(s_ready, 8)
                    act.dma_start(xin[:, :, :], xs[1]).then_inc(x_in, 16)
                for t in range(NT):
                    if r == 1:
                        early = EARLY // NT
                        u_blocks(0, early * t, early, 0)
                    act.wait_ge(shifted, NT * r + t + 1)
                    act.activation(gsel[r][:, t, :], gsel[r][:, t, :], ACT.Exp).then_inc(exped, 1)
                if r == 1:
                    act.wait_ge(sel_turned, 1)
                    act.activation(sel_t[:, 0:2, :].rearrange("p a t -> p (a t)"), ps[:, 6, :], ACT.Copy)
                    act.activation(sel_t[:, 2, :], ps[:, 7, 0:TOK], ACT.Copy)
                leave(act, "act"); n += 1

            yr = [y[r].rearrange("(t p) d -> p t d", p=P) for r in range(REQ)]
            for h in range(HALVES):
                enter(act, "act", n)
                if h == 0:
                    act.wait_ge(dots_done, 1)
                    act.activation(coef[:, :, :], dots[:, :, :], ACT.Gelu).then_inc(gelu_done, 1)
                    act.dma_start(acc[:, :, :], yr[0]).then_inc(x1_back, 16)
                else:
                    act.wait_ge(y_half, 16)
                k0 = 0 if h else EARLY
                with act.Fori(0, TOK // (2 * SPAN)) as i:
                    for c in range(2):
                        act.wait_ge(picks_free, i * 2 + (TOK // SPAN * h + c + 3))
                        act.activation(coefs[:, k0:, bass.ds(i * (2 * SPAN) + SPAN * c, SPAN)],
                                       ps[:, c, :].rearrange("p (m k) -> p k m", m=SPAN)[:, k0:, :], ACT.Copy).then_inc(spread, 1)
                leave(act, "act"); n += 1

                enter(act, "act", n)
                b0 = 0 if h else EARLY
                u_blocks(h, b0, HB - b0, 1)
                leave(act, "act"); n += 1

                enter(act, "act", n)
                g0 = table_g0[h][1]

                def blocks(i):
                    for j in range(2 * BODY):
                        split_hi(i * (2 * BODY) + (g0 + j), j)
                        if j % 2 == 0:
                            act.activation(c_hi[:, j // 2 % 2, :],
                                           coefs[:, bass.ds(i * BODY + j // 2, 1), :].rearrange("p a t -> p (a t)"),
                                           ACT.Copy).then_inc(c_hi_ready, 1)
                with act.Fori(0, HB // BODY - 1) as i:
                    blocks(i)
                act.wait_ge(c_hi_ready, HB * (h + 1) - BODY)
                act.wait_ge(c_lo_ready, HB * (h + 1) - BODY)
                act.dma_start(total[:, :, :], yr[1]).then_inc(x1_in1, 16)
                blocks(HB // BODY - 1)
                leave(act, "act"); n += 1

                enter(act, "act", n)
                act.wait_ge(total_done, h + 1)
                act.dma_start(yr[1], total[:, :, :]).then_inc(y_half, 16)
                leave(act, "act"); n += 1
            act.wait_ge(acc_done, 1)
            act.dma_start(yr[0], acc[:, :, :]).then_inc(y_out, 16)
            act.wait_ge(y_out, 16 * (REQ + 1))
            act.wait_ge(y_half, 16 * HALVES)

        @block.vector
        def _(dve):
            own, qk_own = Counter(dve_own), Counter(dve_qk_own)
            dve.sem_inc(used, ROWS)
            dve.sem_inc(copied, 1)
            dve.sem_inc(roped, 1)
            dve.memset(zeros[:, :], 0.0).then_inc(zero_ready, 1)
            dve.memset(stat[:, 12:13], EPS).then_inc(eps_ready, 1)

            def split_lo(g_, j):
                dve.wait_ge(hi_ready, g_ + 1)
                dve.tensor_tensor(w_lo[:, j % 2, :, :], w[:, j % RING, :, :], w_hi[:, j % 2, :, :].bitcast(F32),
                                  ALU.subtract).then_inc(lo_ready, 1)

            def turn(K, j, table, t):
                first = table
                n_ = K * 8 + (8 * GROUPS * first + j)
                if j == 0:
                    dve.wait_ge(copied, K + (GROUPS * first + 1))
                    if table:
                        dve.wait_ge(used, n_ + ROWS)
                        dve.tensor_copy(stage_d[:, :], coef[:, :, :].rearrange("p t k -> p (t k)")[:, bass.ds(K * 8, 8)]).then_inc(copied, 1)
                        dve.wait_ge(copied, K + (GROUPS * first + 2))
                row = rows[:, j % ROWS, :]
                dve.wait_ge(row_in[j % ROWS], K * (16 * 8 // ROWS) + (16 * 8 // ROWS * GROUPS * first + 16 * (j // ROWS + 1)))
                if table == 0:
                    dve.tensor_tensor_reduce(out=row, in0=row, in1=h2[0][:, t, :], scale=1.0, scalar=0.0, op0=ALU.mult,
                                             op1=ALU.add, accum_out=stage_d[:, j:j + 1]).then_inc(used, 1)
                else:
                    dve.wait_ge(used, n_ + ROWS)
                    dve.scalar_tensor_tensor(acc[:, t, :], row, stage_d[:, j:j + 1], acc[:, t, :],
                                             ALU.mult, ALU.add).then_inc(used, 1)
                if j in (3, 7):
                    h = j // 4
                    dve.wait_ge(ticked, K * 4 + (4 * GROUPS * first + 2 * h + 2))
                    dve.tensor_copy(stage_i[:, 4 * h:4 * h + 4],
                                    eidx[:, bass.ds(K * 8 + (8 * GROUPS * table + 8 + 4 * h), 4)])
                if j == 7 and table == 0:
                    dve.wait_ge(used, n_ + ROWS + 1)
                    dve.tensor_copy(dots[:, :, :].rearrange("p t k -> p (t k)")[:, bass.ds(K * 8, 8)], stage_d[:, :]).then_inc(copied, 1)

            def split_turned(g_, j):
                dve.wait_ge(hi_ready, g_ + 1)
                dve.tensor_tensor(w_lo[:, j % 2, :, :], ps[:, 2 * (j % 2):2 * (j % 2) + 2, :],
                                  w_hi[:, j % 2, :, :].bitcast(F32), ALU.subtract).then_inc(lo_ready, 1)

            early_slabs = [0]

            def beside(r, m=1):
                for _ in range(m if r == 1 else 0):
                    j = early_slabs[0]
                    split_turned(table_g0[0][0] + j, j)
                    if j % 4 != 3:
                        turns(1, 1)
                    early_slabs[0] += 1

            taken = [0]

            def turns(r, m):
                if r == 1:
                    for _ in range(m):
                        turn(taken[0] // 8, taken[0] % 8, 0, taken[0] // SEL)
                        taken[0] += 1

            def stream(ph, r):
                k0 = taken[0] // 8
                with dve.Fori(0, ph["pairs"]) as i:
                    for j in range(2 * SPC):
                        split_lo(i * (2 * SPC) + (ph["g0"] + j), j)
                        if r == 1 and j % 2:
                            turn(i + k0, j // 2, 0, 8 * k0 // SEL)
                if r == 1:
                    taken[0] += 8 * ph["pairs"]

            def inverse_root(own, mean, root, out, tmp):
                own.after(dve, dve.reciprocal(out, root))
                own.after(dve, dve.tensor_tensor(tmp, out, out, ALU.mult))
                own.after(dve, dve.tensor_tensor(tmp, tmp, mean, ALU.mult))
                own.after(dve, dve.tensor_scalar(tmp, tmp, -0.5, 1.5, ALU.mult, ALU.add))
                own.after(dve, dve.tensor_tensor(out, out, tmp, ALU.mult))

            def normalise(k, src, dst):
                dve.wait_ge(sum_ready, NT * (k + 1))
                dve.tensor_scalar(stat[:, 2:4], stat[:, 0:2], 1.0 / D, EPS, ALU.mult, ALU.add).then_inc(mean_ready, 1)
                dve.wait_ge(mean_ready, k + 1)
                dve.wait_ge(root_ready, k + 1)
                inverse_root(own, stat[:, 2:4], stat[:, 4:6], stat[:, 6:8], stat[:, 8:10])
                for t in range(NT):
                    dve.scalar_tensor_tensor(dst[:, t, :], src[:, t, :], stat[:, 6 + t:7 + t], gvec[:, :],
                                             ALU.mult, ALU.mult).then_inc(normed, 1)
                for t in range(NT):
                    for q in range(4):
                        dve.wait_ge(turn_hi, k * 8 + t * 4 + q + 1)
                        dve.tensor_tensor(ht_lo[:, 4 * q:4 * q + 4, t * P:(t + 1) * P],
                                          ps[:, 4 + q, :].rearrange("p (k t) -> p k t", k=4),
                                          ht_hi[:, 4 * q:4 * q + 4, t * P:(t + 1) * P].bitcast(F32),
                                          ALU.subtract).then_inc(turn_lo, 1)

            n = 0
            dve.wait_ge(consts_in, 96)
            for r in range(REQ):
                ph = phases[r]
                enter(dve, "dve", n)
                dve.wait_ge(g_in, 16 * (r + 1))
                normalise(2 * r, xin, x1)
                leave(dve, "dve"); n += 1

                enter(dve, "dve", n)
                k0 = taken[0] // 8

                def pair(i, tiles, beside):
                    for j in range(2 * SPC):
                        split_lo(i * (2 * SPC) + (ph["qkv"]["g0"] + j), j)
                        if r == 1 and j % 2:
                            turn(i + k0, j // 2, 0, 8 * k0 // SEL)
                        if j >= SPC and tiles:
                            norm_step(i, j - SPC, tiles, beside)

                def norm_step(i, j, tiles, rotation):
                    heads = 4 if tiles == 2 else B_KV
                    m = tiles * NT * heads
                    if j == 0:
                        dve.wait_ge(rooted, i + QK_PAIRS * r)
                        qk_own.after(dve, dve.tensor_scalar(ss[:, 0:m], ss[:, 0:m], 1.0 / DH, EPS, ALU.mult, ALU.add))
                        inverse_root(qk_own, ss[:, 0:m], root[:, 0:m], rs[:, 0:m], rtmp[:, 0:m])
                    c, t = (j - 1) // 2, (j - 1) % 2
                    if 0 <= c < tiles:
                        for h in range(heads):
                            v = tile_of(i, c)[:, t, h * DH:(h + 1) * DH]
                            k = (c * NT + t) * heads + h
                            ins = dve.scalar_tensor_tensor(v, v, rs[:, k:k + 1], gain[:, rotation(c)[0], :], ALU.mult, ALU.mult)
                        qk_own.after(dve, ins)
                    if j >= 5 and j - 5 < tiles:
                        rotation(j - 5)[1](tile_of(i, j - 5), heads)
                    if j == 7:
                        dve.drain().then_inc(roped, 1)

                def tile_of(i, c):
                    return raw[:, bass.ds(i * 2 + (c - 2), 1), :, :].rearrange("p a t d -> p (a t) d")

                def rotate(first, second, cos, sin, tmp):
                    dve.tensor_tensor(tmp(0), first, cos, ALU.mult)
                    dve.tensor_tensor(tmp(1), second, sin, ALU.mult)
                    dve.tensor_tensor(tmp(2), second, cos, ALU.mult)
                    qk_own.after(dve, dve.tensor_tensor(tmp(3), first, sin, ALU.mult))
                    dve.tensor_tensor(first, tmp(0), tmp(1), ALU.subtract)
                    qk_own.after(dve, dve.tensor_tensor(second, tmp(2), tmp(3), ALU.add))

                def rotate_a(v, heads):
                    v = v.rearrange("p t (h d) -> p t h d", d=DH)
                    cs = [rope_a[:, k, :, :].unsqueeze(2).to_broadcast([P, NT, heads, ROT]) for k in range(2)]
                    rotate(v[:, :, :, 0:ROT], v[:, :, :, ROT:2 * ROT], cs[0], cs[1],
                           lambda k: rt[:, k, 0:NT * heads * ROT].rearrange("p (t h d) -> p t h d", h=heads, d=ROT))

                def rotate_b(v, heads):
                    for t in range(NT):
                        vt = v[:, t, 0:heads * DH].rearrange("p (h s d) -> p h s d", s=2, d=64)
                        cs = [rope_b[:, k, t, :, :].unsqueeze(1).to_broadcast([P, heads, 2, 32]) for k in range(2)]
                        rotate(vt[:, :, :, 0:32], vt[:, :, :, 32:64], cs[0], cs[1],
                               lambda k: rt[:, k, 0:heads * 64].rearrange("p (h s d) -> p h s d", s=2, d=32))

                pair(0, 0, None)
                start = qk_own.n
                with dve.Fori(1, A_GROUPS + 1) as i:
                    per = QK_OPS
                    qk_own.base = i * per - per
                    pair(i, 2, lambda c: (c, rotate_a))
                assert qk_own.n == start + per
                qk_own.base, qk_own.n = 0, start + A_GROUPS * per
                pair(4, 2, lambda c: (2, rotate_b))
                pair(5, 1, lambda c: (3, rotate_b))
                if r == 1:
                    taken[0] += 8 * ph["qkv"]["pairs"]
                leave(dve, "dve"); n += 1

                enter(dve, "dve", n)

                def maxima(u):
                    dve.wait_ge(sc_ready, N_UNITS * r + u + 1)
                    b0 = 2 * (u % 2)
                    if N_UNITS * r + u >= 2:
                        dve.wait_ge(p_turned, N_UNITS * r + u - 1)
                    if u < 8:
                        own.after(dve, dve.tensor_tensor_reduce(
                            out=prob[:, u % 2, :], in0=ps[:, b0:b0 + 2, :].rearrange("p b c -> p (b c)")[:, 0:768],
                            in1=mask[:, u % 2, :], scale=1.0, scalar=LOWEST, op0=ALU.add, op1=ALU.max, accum_out=ust[:, u, 0:1]))
                        dve.tensor_scalar(ust[:, u, 2:3], ust[:, u, 0:1], -SCALE, None, ALU.mult).then_inc(sc_max, 1)
                    else:
                        own.after(dve, dve.tensor_reduce(ust[:, u, 0:2], ps[:, b0, :].rearrange("p (t k) -> p t k", t=NT), AX.X, ALU.max))
                        dve.tensor_scalar(ust[:, u, 2:4], ust[:, u, 0:2], -SCALE, None, ALU.mult).then_inc(sc_max, 1)

                def rest(u):
                    if u >= 8 or u % 2 == 1:
                        o_ = out_of(u)
                        dve.wait_ge(o_hi, N_OUT * r + o_ + 1)
                        dve.tensor_tensor(ot_lo[:, o_, :], ps[:, 6 + o_ % 2, 0:TOK], ot_hi[:, o_, :].bitcast(F32),
                                          ALU.subtract).then_inc(o_lo, 1)

                turns(r, 6)
                maxima(0)
                for u in range(N_UNITS):
                    if u:
                        turns(r, 2)
                    if u + 1 < N_UNITS:
                        maxima(u + 1)
                    turns(r, 3 if u < 12 else 2)
                    dve.wait_ge(exp_done, N_UNITS * r + u + 1)
                    if u < 8:
                        own.after(dve, dve.reciprocal(ust[:, u, 6:7], ust[:, u, 4:5]))
                        dve.tensor_scalar(prob[:, u % 2, :], prob[:, u % 2, :], ust[:, u, 6:7], None, ALU.mult).then_inc(p_ready, 1)
                    else:
                        own.after(dve, dve.reciprocal(ust[:, u, 6:8], ust[:, u, 4:6]))
                        for t in range(NT):
                            ins = dve.tensor_scalar(prob[:, u % 2, t * TOK:(t + 1) * TOK], prob[:, u % 2, t * TOK:(t + 1) * TOK],
                                                    ust[:, u, 6 + t:7 + t], None, ALU.mult)
                        ins.then_inc(p_ready, 1)
                    if u:
                        rest(u - 1)
                rest(N_UNITS - 1)
                leave(dve, "dve"); n += 1

                enter(dve, "dve", n)
                stream(ph["gate"], r)
                leave(dve, "dve"); n += 1

                enter(dve, "dve", n)
                for ct in range(4):
                    for k in range(BR_SLABS):
                        gg = ph["branch"]["g0"] + BR_SLABS * ct + k
                        split_lo(gg, gg % RING)
                        turns(r, 0 if k % 3 == 2 else 1)
                    for side in range(2):
                        dve.wait_ge(slab_done, ph["branch"]["g0"] + BR_SLABS * ct + (BR_A, BR_SLABS)[side] + 2)
                        if ct and side == 0:
                            dve.wait_ge(merged_hi, 4 * r + ct)
                        dve.tensor_tensor((m1, m2)[side][:, :, :].rearrange("p a t -> p (a t)"),
                                          ps[:, 2 * side:2 * side + 2, :].rearrange("p b c -> p (b c)"),
                                          sg[:, KC * side + 4 * ct:KC * side + 4 * ct + 4, :].rearrange("p a t -> p (a t)"),
                                          ALU.mult).then_inc(acc_free, 1)
                    dve.wait_ge(acc_free, 2 + ph["branch"]["a0"] + 2 * ct + 2)
                    dve.tensor_tensor(m1[:, :, :], m1[:, :, :], m2[:, :, :], ALU.add).then_inc(merged, 1)
                    dve.wait_ge(merged_hi, 4 * r + ct + 1)
                    dve.tensor_tensor(ht_lo[:, 4 * ct:4 * ct + 4, :], m1[:, :, :], ht_hi[:, 4 * ct:4 * ct + 4, :].bitcast(F32), ALU.subtract)
                leave(dve, "dve"); n += 1

                enter(dve, "dve", n)
                dve.wait_ge(xres_in, 16 * (r + 1))
                dve.wait_ge(g2_in, 16 * (r + 1))

                def residual(ct):
                    dve.wait_ge(slab_done, ph["out"]["g0"] + SPC * (ct + 1) + 2)
                    dve.tensor_tensor(x1[:, :, ct * CT:(ct + 1) * CT], ps[:, 2 * (ct % 2):2 * (ct % 2) + 2, :],
                                      xin[:, :, ct * CT:(ct + 1) * CT], ALU.add).then_inc(acc_free, 1)
                for i in range(4 * SPC):
                    split_lo(ph["out"]["g0"] + i, i % RING)
                    turns(r, i % 2)
                    if i % SPC == 3 and i > SPC:
                        residual(i // SPC - 1)
                residual(3)
                dve.wait_ge(acc_free, 2 + ph["out"]["a0"] + 4)
                normalise(2 * r + 1, x1, h2[r])
                leave(dve, "dve"); n += 1

                enter(dve, "dve", n)
                stream(ph["pq"], r)
                leave(dve, "dve"); n += 1

                enter(dve, "dve", n)
                if r == 0:
                    own.after(dve, dve.memset(eidx[:, 2 * NT * SEL:], 0))
                for t in range(NT):
                    dve.wait_ge(s_out, 8 * r + 4 * t + 4)

                    def top16(values, val, idx, m):
                        def each(step):
                            for k in range(m):
                                ins = step(k)
                                if k % (m // 2) == m // 2 - 1:
                                    beside(r)
                            own.after(dve, ins)
                        each(lambda k: dve.max(val(k)[:, 0:8], values(k)))
                        each(lambda k: dve.max_index(idx(k)[:, 0:8], val(k)[:, 0:8], values(k)))
                        each(lambda k: dve.match_replace(values(k), val(k)[:, 0:8], values(k), LOWEST))
                        each(lambda k: dve.max(val(k)[:, 8:16], values(k)))
                        each(lambda k: dve.max_index(idx(k)[:, 8:16], val(k)[:, 8:16], values(k)))

                    top16(lambda k: s[:, t, k, :], lambda k: topv[:, k, :], lambda k: topi[:, k, :], 2 * PH)
                    own.after(dve, dve.tensor_copy(topf[:, :, :], topi[:, :, :]))
                    pairs_v = topv[:, :, :].rearrange("p (h c) k -> p h c k", c=2)
                    own.after(dve, dve.tensor_tensor(
                        cand[:, :, :].rearrange("p h (a b) -> p h a b", a=TOPK),
                        pairs_v[:, :, 0, :].unsqueeze(3).to_broadcast([P, PH, TOPK, TOPK]),
                        pairs_v[:, :, 1, :].unsqueeze(2).to_broadcast([P, PH, TOPK, TOPK]), ALU.add))
                    beside(r, 2)
                    top16(lambda k: cand[:, k, :], lambda k: cv[:, k, :], lambda k: ci[:, k, :], PH)
                    dve.tensor_tensor(gsel[r][:, t, :].rearrange("p (h k) -> p h k", h=PH), cv[:, :, :],
                                      cv[:, :, 0:1].to_broadcast([P, PH, TOPK]), ALU.subtract).then_inc(shifted, 1)
                    cflat = ci[:, :, :].rearrange("p h k -> p (h k)")
                    pairs_i = topf[:, :, :].rearrange("p (h c) k -> p h c k", c=2)
                    beside(r)
                    for c in range(2):
                        if c == 0:
                            own.after(dve, dve.tensor_scalar(cpart[:, :], cflat, 4, None, ALU.logical_shift_right))
                        else:
                            own.after(dve, dve.tensor_scalar(cpart[:, :], cflat, 15, None, ALU.bitwise_and))
                        own.after(dve, dve.tensor_copy(cpf[:, :], cpart[:, :]))
                        own.after(dve, dve.tensor_tensor(eq[:, :, :], cpf[:, :].unsqueeze(2).to_broadcast([P, SEL, TOPK]),
                                                         iota[:, 0:TOPK].unsqueeze(1).to_broadcast([P, SEL, TOPK]), ALU.is_equal))
                        beside(r, 1)
                        eqh = eq[:, :, :].rearrange("p (h k) a -> p h k a", h=PH)
                        own.after(dve, dve.tensor_tensor(eqh, eqh, pairs_i[:, :, c, :].unsqueeze(2).to_broadcast([P, PH, TOPK, TOPK]),
                                                         ALU.mult))
                        beside(r, 2)
                        own.after(dve, dve.tensor_reduce(keys[:, c, t, :], eq[:, :, :], AX.X, ALU.add))
                        beside(r)
                    if r == 0:
                        own.after(dve, dve.scalar_tensor_tensor(esum[:, :], keys[:, 0, t, :], float(NKEYS), keys[:, 1, t, :], ALU.mult, ALU.add))
                        for table in range(2):
                            k = (NT * table + t) * SEL
                            own.after(dve, dve.tensor_copy(eidx[:, k:k + SEL], esum[:, :]))
                    beside(r, (EARLY * 2 // NT) * (t + 1) - early_slabs[0])
                    dve.wait_ge(exped, NT * r + t + 1)
                    gv = gsel[r][:, t, :].rearrange("p (h k) -> p h k", h=PH)
                    own.after(dve, dve.tensor_reduce(gsum[:, :], gv, AX.X, ALU.add))
                    own.after(dve, dve.reciprocal(gsum[:, :], gsum[:, :]))
                    own.after(dve, dve.tensor_tensor(gv, gv, gsum[:, :].unsqueeze(2).to_broadcast([P, PH, TOPK]), ALU.mult))
                if r == 1:
                    dve.drain().then_inc(sel_ready, 1)
                else:
                    dve.tensor_copy(stage_i[:, :], eidx[:, 0:8]).then_inc(staged, 1)
                leave(dve, "dve"); n += 1

            assert taken[0] == NT * SEL
            dve.wait_ge(copied, GROUPS + 1)
            dve.drain().then_inc(dots_done, 1)
            for h in range(HALVES):
                enter(dve, "dve", n)
                if h == 0:
                    dve.wait_ge(gelu_done, 1)
                    own.after(dve, dve.tensor_tensor(coef[:, :, :], coef[:, :, :], gsel[0][:, :, :], ALU.mult))
                    own.after(dve, dve.tensor_copy(weight_split[:, 0, :], sel_t[:, 2, :]))
                    own.after(dve, dve.tensor_tensor(weight_split[:, 1, :], sel_t[:, 2, :], weight_split[:, 0, :].bitcast(F32), ALU.subtract))
                    dve.wait_ge(x1_back, 16)

                def spans(i, first=False):
                    for j in range(8):
                        c, span = j % 2, bass.ds(i * (8 * SPAN) + SPAN * j, SPAN)
                        dve.wait_ge(picks_free, i * 8 + (TOK // SPAN * h + j + 1))
                        dve.tensor_tensor(match1[:, c, :, :], iota[:, HB * h:HB * h + HB].unsqueeze(1).to_broadcast([P, SPAN, HB]),
                                          sel_t[:, 0, span].unsqueeze(2).to_broadcast([P, SPAN, HB]),
                                          ALU.is_equal).then_inc(matched, 1)
                        dve.tensor_tensor(pick2[:, c, :, :], iota[:, :].unsqueeze(1).to_broadcast([P, SPAN, NKEYS]),
                                          sel_t[:, 1, span].unsqueeze(2).to_broadcast([P, SPAN, NKEYS]), ALU.is_equal)
                        dve.wait_ge(matched, i * 8 + (TOK // SPAN * h + j + 1))
                        dve.tensor_tensor(pick1[:, c, :, :, :], match1[:, c, :, :].unsqueeze(1).to_broadcast([P, 2, SPAN, HB]),
                                          weight_split[:, :, span].bitcast(F32).unsqueeze(3).to_broadcast([P, 2, SPAN, HB]),
                                          ALU.mult).then_inc(picks_ready, 1)
                        if h == 0:
                            if not (first and j == 0):
                                weigh_early(i * 8 + (j - 1), 1 - c)
                            turn(i, j, 1, 0)

                def weigh_early(span, c):
                    dve.wait_ge(spread, span + 3)
                    cs = coefs[:, 0:EARLY, bass.ds(span * SPAN, SPAN)]
                    dve.tensor_tensor(cs, cs, ps[:, c, :].rearrange("p (m k) -> p k m", m=SPAN)[:, 0:EARLY, :], ALU.mult).then_inc(weighed, 1)

                if h == 0:
                    spans(0, True)
                    with dve.Fori(1, TOK // (8 * SPAN)) as i:
                        spans(i)
                    weigh_early(TOK // SPAN - 1, 1)
                else:
                    with dve.Fori(0, TOK // (8 * SPAN)) as i:
                        spans(i)
                leave(dve, "dve"); n += 1

                def table(K0, rounds, count, n_turns, slab):
                    per, per_turns = 2 * count // rounds, n_turns // rounds
                    with dve.Fori(0, rounds) as i:
                        k = 0
                        for j in range(per):
                            slab(i, per // 2, j)
                            while k < (j + 1) * per_turns // per:
                                turn(i * (per_turns // 8) + (K0 + k // 8), k % 8, 1, h)
                                k += 1

                enter(dve, "dve", n)
                b0 = 0 if h else EARLY
                K1 = GROUPS // HALVES * h + (0 if h else G_TURNS // 8)

                def weigh(b, par):
                    dve.wait_ge(a_free, b + (HB * h + b0 + 3))
                    cb = coefs[:, bass.ds(b + b0, 1), :].rearrange("p a t -> p (a t)")
                    dve.tensor_tensor(cb, cb, ge[:, par, :], ALU.mult).then_inc(c_made, 1)

                def u_slab(i, blocks, j):
                    split_turned(i * (2 * blocks) + (table_g0[h][0] + 2 * b0 + j), j)
                    if j % 2 and j > 1:
                        weigh(i * blocks + (j // 2 - 1), (j // 2 - 1) % 2)
                    if j == 2 * blocks - 1:
                        weigh(i * blocks + j // 2, j // 2 % 2)
                table(K1, 2, HB - b0, U_TURNS[h], u_slab)
                leave(dve, "dve"); n += 1

                enter(dve, "dve", n)

                def v_slab(i, blocks, j):
                    split_lo(i * (2 * blocks) + (table_g0[h][1] + j), j)
                    if j % 2 == 0:
                        dve.wait_ge(c_hi_ready, i * blocks + (HB * h + j // 2 + 1))
                        dve.tensor_tensor(c_lo[:, j // 2 % 2, :],
                                          coefs[:, bass.ds(i * blocks + j // 2, 1), :].rearrange("p a t -> p (a t)"),
                                          c_hi[:, j // 2 % 2, :].bitcast(F32), ALU.subtract).then_inc(c_lo_ready, 1)
                table(K1 + U_TURNS[h] // 8, 2, HB, V_TURNS, v_slab)
                leave(dve, "dve"); n += 1

                enter(dve, "dve", n)
                dve.wait_ge(x1_in1, 16 * (h + 1))
                for t in range(NT):
                    for c in range(4):
                        ins = dve.tensor_tensor(total[:, t, c * CT:(c + 1) * CT], ps[:, 4 * t + c, :], total[:, t, c * CT:(c + 1) * CT], ALU.add)
                ins.then_inc(total_done, 1)
                leave(dve, "dve"); n += 1
            dve.drain().then_inc(acc_done, 1)

        @block.tensor
        def _(pe):
            pe.wait_ge(consts_in, 96)
            pe.sem_inc(slab_done, 2)
            pe.sem_inc(acc_free, 2)
            for sem in (picks_free, spread, weighed, a_free, c_made):
                pe.sem_inc(sem, 2)

            def slab(g_, j, ks, form, lhs, b0, first, last):
                hi, lo = lhs
                for part, (wt, other) in enumerate(((w_hi, hi), (w_hi, lo), (w_lo, hi))):
                    if part == 0:
                        pe.wait_ge(hi_ready, g_ + 1)
                    if part == 2:
                        pe.wait_ge(lo_ready, g_ + 1)
                    for kk in range(SK):
                        k = ks + kk
                        start = first and part == 0 and kk == 0
                        stop = last and part == 2 and kk == SK - 1
                        if form == "rows":
                            for t in range(NT):
                                ins = pe.matmul(ps[:, b0 + t, :], other[:, k, t * P:(t + 1) * P], wt[:, j % 2, kk, :],
                                                start=start, stop=stop)
                        else:
                            for q in range(4):
                                ins = pe.matmul(ps[:, b0 + q // 2, (q % 2) * TOK:(q % 2 + 1) * TOK],
                                                wt[:, j % 2, kk, q * P:(q + 1) * P], other[:, k, :],
                                                start=start and q % 2 == 0, stop=stop, skip_group_check=True)
                ins.then_inc(slab_done, 1)
                return ins

            def stream(ph, form):
                def pair(i):
                    for c in range(2):
                        pe.wait_ge(acc_free, i * 2 + (ph["a0"] + c + 1))
                        for j in range(SPC):
                            slab(i * (2 * SPC) + (ph["g0"] + SPC * c + j), j, SK * j, form, (ht_hi, ht_lo), 2 * c,
                                 j == 0, j == SPC - 1)
                with pe.Fori(0, ph["pairs"]) as i:
                    pair(i)

            def normalise(k, src):
                for t in range(NT):
                    pe.wait_ge(normed, k * NT + t + 1)
                    for q in range(4):
                        if t:
                            pe.wait_ge(turn_lo, k * 8 + q + 1)
                        for c in range(4):
                            ins = pe.transpose(ps[:, 4 + q, c * P:(c + 1) * P], src[:, t, (4 * q + c) * P:(4 * q + c + 1) * P], ident[:, :])
                        ins.then_inc(turned, 1)

            def u_blocks(h, b0, count):
                g0 = table_g0[h][0] + 2 * b0

                def turn_block(G, j):
                    pe.wait_ge(w_loaded[j % RING], (G + (g0 - j % RING)) * (16 // RING) + 16)
                    pe.wait_ge(lo_ready, G + (g0 - 1))
                    for k in range(8):
                        ins = pe.transpose(ps[:, 2 * (j % 2) + k // 4, k % 4 * P:(k % 4 + 1) * P],
                                           w[:, j % RING, k // 4, k % 4 * P:(k % 4 + 1) * P], ident[:, :])
                    ins.then_inc(u_turned, 1)

                def blocks(i, last=False):
                    for j in range(2 * BODY):
                        if not (last and j == 2 * BODY - 1):
                            turn_block(i * (2 * BODY) + (j + 1), j + 1)
                        c, b = j % 2, j // 2
                        if c == 0:
                            pe.wait_ge(a_free, i * BODY + (HB * h + b0 + b + 1))
                        for part, (wt, other) in enumerate(((w_hi, ht_hi), (w_hi, ht_lo), (w_lo, ht_hi))):
                            if part == 0:
                                pe.wait_ge(hi_ready, i * (2 * BODY) + (g0 + j + 1))
                            if part == 2:
                                pe.wait_ge(lo_ready, i * (2 * BODY) + (g0 + j + 1))
                            for k in range(8):
                                ins = pe.matmul(ps[:, 4 + b % 2, 0:TOK], wt[:, j % 2, k // 4, k % 4 * P:(k % 4 + 1) * P],
                                                other[:, 8 * c + k, :], start=(c == 0 and part == 0 and k == 0),
                                                stop=(c == 1 and part == 2 and k == 7))
                        ins.then_inc(slab_done, 1)
                turn_block(0, 0)
                with pe.Fori(0, count // BODY - 1) as i:
                    blocks(i)
                blocks(count // BODY - 1, True)

            n = 0
            for r in range(REQ):
                ph = phases[r]
                enter(pe, "pe", n)
                normalise(2 * r, x1)
                leave(pe, "pe"); n += 1

                enter(pe, "pe", n)
                stream(ph["qkv"], "rows")
                leave(pe, "pe"); n += 1

                enter(pe, "pe", n)
                pe.wait_ge(roped, QK_PAIRS * (r + 1) + 1)
                for u in range(N_QK):
                    nh = 4 if u < 8 else 2
                    if u >= 2:
                        pe.wait_ge(qk_out, 9 * r + u - 1)
                    b0 = 4 * (u % 2)
                    for h in range(nh):
                        for t in range(NT):
                            ins = pe.transpose(ps[:, b0 + h // 2, (h % 2) * TOK + t * P:(h % 2) * TOK + (t + 1) * P],
                                               raw[:, u, t, h * DH:(h + 1) * DH], ident[:, :])
                    ins.then_inc(qk_turned, 1)
                pe.wait_ge(qk_out, 9 * (r + 1))

                def scores(u):
                    uu = N_UNITS * r + u
                    b0 = 2 * (u % 2)
                    if u >= 2:
                        pe.wait_ge(exp_done, uu - 1)
                    if u < 8:
                        hh, t = u // 2, u % 2
                        for g_ in range(A_GROUPS):
                            ins = pe.matmul(ps[:, b0 + g_ // 2, (g_ % 2) * TOK:(g_ % 2 + 1) * TOK],
                                            qkt(2 * g_, hh)[:, t * P:(t + 1) * P], qkt(2 * g_ + 1, hh), start=True, stop=True)
                    else:
                        qh = u - 8
                        for t in range(NT):
                            ins = pe.matmul(ps[:, b0, t * TOK:(t + 1) * TOK], qkt(6 + qh // 4, qh % 4)[:, t * P:(t + 1) * P],
                                            qkt(8, qh // 4), start=True, stop=True)
                    ins.then_inc(sc_ready, 1)

                scores(0)
                scores(1)
                for u in range(N_UNITS):
                    uu = N_UNITS * r + u
                    pe.wait_ge(p_ready, uu + 1)
                    if uu:
                        pe.wait_ge(pt_ready, uu)
                    if u < 8:
                        for k in range(6):
                            ins = pe.transpose(ps[:, 4 + k // 4, (k % 4) * P:(k % 4 + 1) * P],
                                               prob[:, u % 2, k * P:(k + 1) * P], ident[:, :])
                    else:
                        for t in range(NT):
                            for k in range(2):
                                ins = pe.transpose(ps[:, 4, k * TOK + t * P:k * TOK + (t + 1) * P],
                                                   prob[:, u % 2, t * TOK + k * P:t * TOK + (k + 1) * P], ident[:, :])
                    ins.then_inc(p_turned, 1)
                    if u + 2 < N_UNITS:
                        scores(u + 2)
                    if u >= 8 or u % 2 == 1:
                        o_ = out_of(u)
                        pe.wait_ge(pt_ready, uu + 1)
                        if o_ >= 2:
                            pe.wait_ge(o_lo, N_OUT * r + o_ - 1)
                        if u < 8:
                            vals = [raw[:, N_QK + k // 2, k % 2, o_ * DH:(o_ + 1) * DH] for k in range(6)]
                        else:
                            kv = 256 + (u - 8) // 4 * DH
                            vals = [raw[:, N_QK - 1, k, kv:kv + DH] for k in range(2)]
                        for k, val in enumerate(vals):
                            ins = pe.matmul(ps[:, 6 + o_ % 2, 0:TOK], val, pt[:, o_ % 2, k, :], start=(k == 0), stop=(k == len(vals) - 1))
                        ins.then_inc(pv_ready, 1)
                leave(pe, "pe"); n += 1

                enter(pe, "pe", n)
                stream(ph["gate"], "columns")
                leave(pe, "pe"); n += 1

                enter(pe, "pe", n)
                gg = ph["branch"]["g0"]
                for ct in range(4):
                    for side, (k0, ns) in enumerate(((0, BR_A), (4, BR_SLABS - BR_A))):
                        pe.wait_ge(acc_free, ph["branch"]["a0"] + 2 * ct + side + 1)
                        for j in range(ns):
                            slab(gg, gg, k0 + SK * j, "columns", (ot_hi, ot_lo), 2 * side, j == 0, j == ns - 1)
                            gg += 1
                leave(pe, "pe"); n += 1

                enter(pe, "pe", n)
                stream(ph["out"], "rows")
                normalise(2 * r + 1, h2[r])
                leave(pe, "pe"); n += 1

                enter(pe, "pe", n)
                stream(ph["pq"], "columns")
                pe.wait_ge(sk_in, 16 * (r + 1))
                for q in range(4):
                    for c in range(4):
                        ins = pe.transpose(ps[:, 4 + q, c * P:(c + 1) * P], skn[:, 4 * q + c, :], ident[:, :])
                    ins.then_inc(sk_turned, 1)
                leave(pe, "pe"); n += 1

                enter(pe, "pe", n)
                for q in range(8):
                    t, c = q // 4, q % 4
                    for k in range(4):
                        ins = pe.matmul(ps[:, q, k * P:(k + 1) * P], qt[:, 4 * c + k, t * P:(t + 1) * P], skt[:, 4 * c + k, :],
                                        start=True, stop=True)
                    ins.then_inc(s_ready, 1)
                if r == 1:
                    pe.wait_ge(s_out, 8 * REQ)
                    u_blocks(0, 0, EARLY)
                    pe.wait_ge(sel_ready, 1)
                    for k in range(3):
                        for t in range(NT):
                            src = keys[:, k, t, :] if k < 2 else gsel[1][:, t, :]
                            c0 = k % 2 * TOK + t * P
                            ins = pe.transpose(ps[:, 6 + k // 2, c0:c0 + P], src, ident[:, :])
                    ins.then_inc(sel_turned, 1)
                leave(pe, "pe"); n += 1

            pe.wait_ge(zero_ready, 1)
            for h in range(HALVES):
                enter(pe, "pe", n)
                with pe.Fori(0, TOK // 16) as i:
                    for c in range(2):
                        pe.wait_ge(picks_ready, i * 2 + (TOK // SPAN * h + c + 1))
                        pe.wait_ge(spread, i * 2 + (TOK // SPAN * h + c + 1))
                        if h == 0:
                            pe.wait_ge(weighed, i * 2 + (c + 1))
                        for m in range(8):
                            for k in range(2):
                                ins = pe.matmul(ps[:, c, m * HB:(m + 1) * HB], pick2[:, c, m, :], pick1[:, c, k, m, :],
                                                start=(k == 0), stop=(k == 1))
                        ins.then_inc(picks_free, 1)
                leave(pe, "pe"); n += 1

                enter(pe, "pe", n)
                b0 = 0 if h else EARLY
                u_blocks(h, b0, HB - b0)
                leave(pe, "pe"); n += 1

                enter(pe, "pe", n)
                g0 = table_g0[h][1]
                for k in range(8):
                    pe.matmul(ps[:, k, :], zeros[:, 0:P], zeros[:, :], start=True, stop=True)
                with pe.Fori(0, HB // BODY) as i:
                    for j in range(2 * BODY):
                        c, b = j % 2, j // 2
                        for part, (cf, wt) in enumerate(((c_hi, w_hi), (c_lo, w_hi), (c_hi, w_lo))):
                            if part == 0:
                                pe.wait_ge(hi_ready, i * (2 * BODY) + (g0 + j + 1))
                                pe.wait_ge(c_hi_ready, i * BODY + (HB * h + b + 1))
                            if part == 1:
                                pe.wait_ge(c_lo_ready, i * BODY + (HB * h + b + 1))
                            if part == 2:
                                pe.wait_ge(lo_ready, i * (2 * BODY) + (g0 + j + 1))
                            for t in range(NT):
                                for k in range(2):
                                    ins = pe.matmul(ps[:, 4 * t + 2 * c + k, :], cf[:, b % 2, t * P:(t + 1) * P], wt[:, j % 2, k, :],
                                                    start=False, stop=True, skip_group_check=True)
                        ins.then_inc(slab_done, 1)
                leave(pe, "pe"); n += 1
                enter(pe, "pe", n); leave(pe, "pe"); n += 1


def kernel(**inputs):
    import concourse.bacc as bacc
    from concourse.bass_utils import run_bass_kernel_spmd as run

    f = lambda name: np.ascontiguousarray(inputs[name][0])
    rows = lambda v, n: np.ascontiguousarray(np.broadcast_to(v, (n,) + v.shape))
    q = np.arange(TOK)
    near = np.abs(q[:, None] - q[None, :])
    allowed = np.concatenate([near <= 64, near % 4 == 0, near % 16 == 0], axis=1)
    mask = np.where(allowed, 0.0, NEG).astype(np.float32).reshape(NT, P, A_GROUPS * TOK).transpose(1, 0, 2)

    def table(pos, dim, theta):
        inv = np.float32(theta) ** (-(np.arange(0, dim, 2, dtype=np.float32) / np.float32(dim)))
        ang = pos.astype(np.float32)[:, None] * inv[None, :].astype(np.float32)
        return np.stack([np.cos(ang), np.sin(ang)]).astype(np.float32)
    rope_a = table(q, 32, 500000.0).reshape(2, NT, P, ROT).transpose(2, 0, 1, 3)
    rope_b = np.stack([table(q // 64, 64, 10000.0), table(q % 64, 64, 10000.0)], axis=2).reshape(2, NT, P, 2, 32).transpose(2, 0, 1, 3, 4)
    gains = np.stack([f("qn_a"), f("kn_a"), f("qn_b"), f("kn_b")])
    arrays = {
        "x": np.concatenate([inputs["x_prompt"], inputs["x_sample"]], axis=0),
        "g_mix_b": rows(f("g_mix"), P), "g_ffn_b": rows(f("g_ffn"), P), "w_in": f("w_in"), "gains": rows(gains, P),
        "w_br_a": f("w_br_a"), "w_br_b": f("w_br_b"), "w_out": f("w_out"), "w_pq": f("w_pq"),
        "sub_keys": f("sub_keys").reshape(2 * PH, NKEYS, P), "u_emb": f("u_emb"), "v_emb": f("v_emb"),
        "ident_c": np.eye(P, dtype=np.float32), "mask_c": mask, "rope_a_c": rope_a, "rope_b_c": rope_b,
        "iota_c": rows(np.arange(NKEYS, dtype=np.float32), P),
    }
    arrays = {k: np.ascontiguousarray(v) for k, v in arrays.items()}
    nc = bacc.Bacc("TRN2", target_bir_lowering=False, num_devices=1)
    args = [nc.dram_tensor(k, v.shape, F32, kind="ExternalInput").ap() for k, v in arrays.items()]
    y = nc.dram_tensor("y", (REQ, TOK, D), F32, kind="ExternalOutput").ap()
    encoder(nc, *args, y)
    out = run(nc, [arrays], core_ids=[0]).results[0]["y"]
    return out[0:1], out[1:2]
```
